# Optimizing a Trainium2 kernel written in Bass

```python
import math
import jax
import jax.numpy as jnp
from jax import lax
import numpy as np

D_MODEL = 1024
BATCH = 1
SEQ = 512
DEPTH = 1
DEC_BATCH = 8
DEC_SEQ = 1
PAST_LEN = 2048
PAGE_SIZE = 128

H_A = 4
DK_A = 128
DV_A = 128
W_QK_A = H_A * DK_A
W_V_A = H_A * DV_A
C_CONV = 2 * W_QK_A + W_V_A
CONV_W = 4
CHUNK = 64
H_B = 8
HD_B = 64
W_B = H_B * HD_B
MOBA_BLOCK = 256
MOBA_TOPK = 3
Q_BLOCK = 64
ROPE_THETA = 500000.0
ROT_DIM = HD_B // 4
D_FF = 4 * D_MODEL
EPS = 1e-6
SPLIT_SIZES = (C_CONV, W_V_A, H_A, H_A, W_B, W_B, W_B, D_MODEL, D_MODEL)
N_IN = C_CONV + W_V_A + 2 * H_A + 3 * W_B + 2 * D_MODEL
F32 = jnp.float32

kernel_name = 'hybrid_gated_delta_moba_step'

def rmsnorm(x, w):
    xf = x.astype(F32)
    y = xf * lax.rsqrt(jnp.mean(xf * xf, axis=-1, keepdims=True) + EPS) * w.astype(F32)
    return y.astype(x.dtype)

def l2norm(x):
    xf = x.astype(F32)
    return xf * lax.rsqrt(jnp.sum(xf * xf, axis=-1, keepdims=True) + EPS)

def partial_rope(x, pos):
    half = ROT_DIM // 2
    inv_freq = jnp.exp(jnp.arange(half, dtype=F32) * (-2.0 * math.log(ROPE_THETA) / ROT_DIM))
    ang = pos.astype(F32)[:, None] * inv_freq[None, :]
    cos = jnp.cos(ang)[None, :, None, :]
    sin = jnp.sin(ang)[None, :, None, :]
    xf = x.astype(F32)
    x1, x2 = xf[..., :half], xf[..., half:ROT_DIM]
    out = jnp.concatenate([x1 * cos - x2 * sin, x2 * cos + x1 * sin, xf[..., ROT_DIM:]], axis=-1)
    return out.astype(x.dtype)

def in_proj(x, norm_w, w_in):
    h = rmsnorm(x, norm_w) @ w_in
    offsets = np.cumsum(SPLIT_SIZES)[:-1].tolist()
    return jnp.split(h, offsets, axis=-1)

def causal_conv_silu(x, buf, w):
    length = x.shape[1]
    xp = jnp.concatenate([buf.astype(x.dtype), x], axis=1)
    y = xp[:, 0:length] * w[0]
    for i in range(1, CONV_W):
        y = y + xp[:, i:i + length] * w[i]
    return jax.nn.silu(y), xp[:, -(CONV_W - 1):]

def delta_prep(qkv_pre, conv_buf, b_logit, a_logit, conv_w, a_log, dt_bias):
    bsz, length, _ = qkv_pre.shape
    qkv, new_buf = causal_conv_silu(qkv_pre, conv_buf, conv_w)
    q = l2norm(qkv[..., :W_QK_A].reshape(bsz, length, H_A, DK_A)) * (DK_A ** -0.5)
    k = l2norm(qkv[..., W_QK_A:2 * W_QK_A].reshape(bsz, length, H_A, DK_A))
    v = qkv[..., 2 * W_QK_A:].reshape(bsz, length, H_A, DV_A).astype(F32)
    beta = jax.nn.sigmoid(b_logit.astype(F32))
    g = -jnp.exp(a_log.astype(F32)) * jax.nn.softplus(a_logit.astype(F32) + dt_bias.astype(F32))
    return q, k, v, g, beta, new_buf

def gated_delta_chunked(q, k, v, g, beta, s0):
    b, s, h, _ = q.shape
    dv = v.shape[-1]
    nc = s // CHUNK

    def chunks(t):
        t = t.reshape((b, nc, CHUNK, h) + t.shape[3:])
        return jnp.moveaxis(t, 3, 1)

    qc, kc, vc, bc = chunks(q), chunks(k), chunks(v), chunks(beta)
    gc = jnp.cumsum(chunks(g), axis=-1)
    causal = jnp.tril(jnp.ones((CHUNK, CHUNK), bool))
    strict = jnp.tril(jnp.ones((CHUNK, CHUNK), bool), -1)
    decay = jnp.exp(jnp.where(causal, gc[..., :, None] - gc[..., None, :], -jnp.inf))
    kb = kc * bc[..., None]
    a = jnp.where(strict, jnp.einsum('bhnid,bhnjd->bhnij', kb, kc) * decay, 0.0)
    eye = jnp.eye(CHUNK, dtype=a.dtype)
    t_inv = lax.linalg.triangular_solve(a + eye, jnp.broadcast_to(eye, a.shape),
                                        left_side=True, lower=True, unit_diagonal=True)
    u = t_inv @ (vc * bc[..., None])
    w = t_inv @ (kb * jnp.exp(gc)[..., None])
    qk = jnp.where(causal, jnp.einsum('bhnid,bhnjd->bhnij', qc, kc) * decay, 0.0)

    def step(state, xs):
        qi, ki, ui, wi, gi, qki = xs
        v_new = ui - wi @ state
        o = (qi * jnp.exp(gi)[..., None]) @ state + qki @ v_new
        g_last = gi[..., -1:]
        state = state * jnp.exp(g_last)[..., None] + jnp.einsum(
            'bhcd,bhce->bhde', ki * jnp.exp(g_last - gi)[..., None], v_new)
        return state, o

    xs = tuple(jnp.moveaxis(t, 2, 0) for t in (qc, kc, u, w, gc, qk))
    s_fin, o = lax.scan(step, s0, xs)
    o = jnp.moveaxis(jnp.moveaxis(o, 0, 2), 1, 3).reshape(b, s, h, dv)
    return o, s_fin

def gated_delta_recurrent(q, k, v, g, beta, s0):
    def step(state, xs):
        qt, kt, vt, gt, bt = xs
        state = state * jnp.exp(gt)[..., None, None]
        kv = jnp.einsum('bhd,bhde->bhe', kt, state)
        state = state + kt[..., :, None] * ((vt - kv) * bt[..., None])[..., None, :]
        return state, jnp.einsum('bhd,bhde->bhe', qt, state)

    xs = tuple(jnp.moveaxis(t, 1, 0) for t in (q, k, v, g, beta))
    s_fin, o = lax.scan(step, s0, xs)
    return jnp.moveaxis(o, 0, 1), s_fin

def delta_out(o, z, norm_w, w_proj):
    bsz, length = o.shape[:2]
    on = o * lax.rsqrt(jnp.mean(o * o, axis=-1, keepdims=True) + EPS) * norm_w.astype(F32)
    on = on * jax.nn.silu(z.reshape(bsz, length, H_A, DV_A).astype(F32))
    return on.reshape(bsz, length, W_V_A).astype(z.dtype) @ w_proj

def moba_combine(q, q_pos, k_own, v_own, own_pos, ks=None, vs=None, sel_valid=None):
    scale = HD_B ** -0.5
    lo = jnp.einsum('bhqd,bhld->bhql', q, k_own, preferred_element_type=F32) * scale
    lo = jnp.where(own_pos[None, :] <= q_pos[:, None], lo, -jnp.inf)
    if ks is None:
        p = jax.nn.softmax(lo, axis=-1)
        return jnp.einsum('bhql,bhld->bhqd', p.astype(v_own.dtype), v_own, preferred_element_type=F32)
    ls = jnp.einsum('bhqd,bhqkld->bhqkl', q, ks, preferred_element_type=F32) * scale
    if sel_valid is not None:
        ls = jnp.where(sel_valid[..., None], ls, -jnp.inf)
    b, h, nq, nk, bs = ls.shape
    p = jax.nn.softmax(jnp.concatenate([ls.reshape(b, h, nq, nk * bs), lo], axis=-1), axis=-1)
    p_sel = p[..., :nk * bs].reshape(b, h, nq, nk, bs)
    p_own = p[..., nk * bs:]
    return (jnp.einsum('bhqkl,bhqkld->bhqd', p_sel.astype(vs.dtype), vs, preferred_element_type=F32)
            + jnp.einsum('bhql,bhld->bhqd', p_own.astype(v_own.dtype), v_own, preferred_element_type=F32))

def moba_prompt(q, k, v):
    b, s = q.shape[:2]
    nb = -(-s // MOBA_BLOCK)
    pad = nb * MOBA_BLOCK - s

    def blocks(t):
        t = jnp.pad(t, ((0, 0), (0, pad), (0, 0), (0, 0)))
        return t.reshape(b, nb, MOBA_BLOCK, H_B, HD_B).transpose(0, 3, 1, 2, 4)

    kb, vb = blocks(k), blocks(v)
    k_mean = jnp.mean(kb.astype(F32), axis=3)
    kk = min(MOBA_TOPK, nb - 1)
    nq = s // Q_BLOCK
    qc = q.reshape(b, nq, Q_BLOCK, H_B, HD_B).transpose(1, 0, 3, 2, 4)
    b_i = jnp.arange(b)[:, None, None, None]
    h_i = jnp.arange(H_B)[None, :, None, None]

    def one(args):
        ci, qb = args
        start = ci * Q_BLOCK
        blk = start // MOBA_BLOCK
        q_pos = start + jnp.arange(Q_BLOCK)
        k_own = lax.dynamic_index_in_dim(kb, blk, axis=2, keepdims=False)
        v_own = lax.dynamic_index_in_dim(vb, blk, axis=2, keepdims=False)
        own_pos = blk * MOBA_BLOCK + jnp.arange(MOBA_BLOCK)
        if kk == 0:
            return moba_combine(qb, q_pos, k_own, v_own, own_pos)
        scores = jnp.einsum('bhqd,bhnd->bhqn', qb, k_mean, preferred_element_type=F32)
        scores = jnp.where(jnp.arange(nb) < blk, scores, -jnp.inf)
        _, top_i = lax.top_k(scores, kk)
        valid = jnp.arange(kk) < blk
        ks = kb[b_i, h_i, top_i]
        vs = vb[b_i, h_i, top_i]
        return moba_combine(qb, q_pos, k_own, v_own, own_pos, ks, vs, valid)

    o = lax.map(one, (jnp.arange(nq), qc))
    return o.transpose(1, 0, 3, 2, 4).reshape(b, s, W_B)

def moba_sample(q, k_new, v_new, cache_k, cache_v, page_table, layer):
    nbat, length = q.shape[:2]
    ppb = MOBA_BLOCK // PAGE_SIZE
    n_full = PAST_LEN // MOBA_BLOCK
    n_rem = (PAST_LEN - n_full * MOBA_BLOCK) // PAGE_SIZE
    q_pos = PAST_LEN + jnp.arange(length)
    qh = q.transpose(0, 2, 1, 3)
    own_pages = page_table[:, n_full * ppb:n_full * ppb + n_rem]

    def own_rows(pool, new):
        past = pool[layer, own_pages].reshape(nbat, n_rem * PAGE_SIZE, H_B, HD_B).astype(new.dtype)
        return jnp.concatenate([past, new], axis=1).transpose(0, 2, 1, 3)

    k_own = own_rows(cache_k, k_new)
    v_own = own_rows(cache_v, v_new)
    own_pos = n_full * MOBA_BLOCK + jnp.arange(n_rem * PAGE_SIZE + length)
    kk = min(MOBA_TOPK, n_full)
    if kk == 0:
        o = moba_combine(qh, q_pos, k_own, v_own, own_pos)
    else:
        k_past = cache_k[layer, page_table[:, :n_full * ppb]].reshape(nbat, n_full, MOBA_BLOCK, H_B, HD_B)
        k_mean = jnp.mean(k_past.astype(F32), axis=2).transpose(0, 2, 1, 3)
        scores = jnp.einsum('bhqd,bhnd->bhqn', qh, k_mean, preferred_element_type=F32)
        _, top_i = lax.top_k(scores, kk)
        b_i = jnp.arange(nbat)[:, None, None, None]
        h_i = jnp.arange(H_B)[None, :, None, None]
        k_sel = k_past[b_i, top_i, :, h_i]
        phys = page_table[b_i[..., None], top_i[..., None] * ppb + jnp.arange(ppb)]
        v_sel = cache_v[layer, phys, :, h_i[..., None]].reshape(nbat, H_B, length, kk, MOBA_BLOCK, HD_B)
        o = moba_combine(qh, q_pos, k_own, v_own, own_pos, k_sel, v_sel)
    return o.transpose(0, 2, 1, 3).reshape(nbat, length, W_B)

def merge_and_mlp(x, y_a, y_b, gate_a, gate_b, w_out, norm2_w, w_up, w_down):
    mixed = jax.nn.sigmoid(gate_a) * y_a + jax.nn.sigmoid(gate_b) * y_b
    h = x + mixed @ w_out
    u = jnp.square(jax.nn.relu(rmsnorm(h, norm2_w) @ w_up))
    return h + u @ w_down

def setup_inputs(seed: int = 0) -> dict:
    key = jax.random.key(seed)
    keys = jax.random.split(key, 20)
    n_pages = PAST_LEN // PAGE_SIZE
    n_pool = (DEC_BATCH * n_pages * 5) // 4

    def normal(k, shape, scale):
        return jax.random.normal(k, shape, F32) * scale

    def gain(k, shape):
        return 1.0 + normal(k, shape, 0.02)

    perm = jax.random.permutation(keys[4], n_pool)
    page_table = perm[:DEC_BATCH * n_pages].reshape(DEC_BATCH, n_pages).astype(jnp.int32)
    dt = jnp.exp(jax.random.uniform(keys[9], (DEPTH, H_A), F32, math.log(1e-3), math.log(1e-1)))
    return {
        'x_prompt': normal(keys[0], (BATCH, SEQ, D_MODEL), 1.0),
        'x_sample': normal(keys[1], (DEC_BATCH, DEC_SEQ, D_MODEL), 1.0),
        'cache_k': normal(keys[2], (DEPTH, n_pool, PAGE_SIZE, H_B, HD_B), 1.0),
        'cache_v': normal(keys[3], (DEPTH, n_pool, PAGE_SIZE, H_B, HD_B), 1.0),
        'page_table': page_table,
        'state_delta': normal(keys[5], (DEPTH, DEC_BATCH, H_A, DK_A, DV_A), 0.05),
        'state_conv': normal(keys[6], (DEPTH, DEC_BATCH, CONV_W - 1, C_CONV), 1.0),
        'norm1_w': gain(keys[7], (DEPTH, D_MODEL)),
        'w_in': normal(keys[8], (DEPTH, D_MODEL, N_IN), D_MODEL ** -0.5),
        'conv_w': normal(keys[10], (DEPTH, CONV_W, C_CONV), CONV_W ** -0.5),
        'a_log': jnp.log(jax.random.uniform(keys[11], (DEPTH, H_A), F32, 1.0, 16.0)),
        'dt_bias': dt + jnp.log(-jnp.expm1(-dt)),
        'delta_norm_w': gain(keys[12], (DEPTH, DV_A)),
        'w_proj_a': normal(keys[13], (DEPTH, W_V_A, D_MODEL), W_V_A ** -0.5),
        'w_proj_b': normal(keys[14], (DEPTH, W_B, D_MODEL), W_B ** -0.5),
        'w_out': normal(keys[15], (DEPTH, D_MODEL, D_MODEL), D_MODEL ** -0.5),
        'norm2_w': gain(keys[16], (DEPTH, D_MODEL)),
        'w_up': normal(keys[17], (DEPTH, D_MODEL, D_FF), D_MODEL ** -0.5),
        'w_down': normal(keys[18], (DEPTH, D_FF, D_MODEL), D_FF ** -0.5),
        'norm_f_w': gain(keys[19], (D_MODEL,)),
    }

def reference(x_prompt, x_sample, cache_k, cache_v, page_table, state_delta, state_conv,
              norm1_w, w_in, conv_w, a_log, dt_bias, delta_norm_w, w_proj_a, w_proj_b,
              w_out, norm2_w, w_up, w_down, norm_f_w):
    bp, sp = x_prompt.shape[:2]
    bs, ss = x_sample.shape[:2]
    pos_p = jnp.arange(sp, dtype=jnp.int32)
    pos_s = PAST_LEN + jnp.arange(ss, dtype=jnp.int32)
    hp, hs = x_prompt, x_sample
    kp_l, vp_l, dp_l, cp_l = [], [], [], []
    ks_l, vs_l, ds_l, cs_l = [], [], [], []
    for l in range(DEPTH):
        qkv, z, b_lg, a_lg, qb, kb, vb, ga, gb = in_proj(hp, norm1_w[l], w_in[l])
        q, k, v, g, beta, conv_new = delta_prep(qkv, jnp.zeros((bp, CONV_W - 1, C_CONV), hp.dtype),
                                                b_lg, a_lg, conv_w[l], a_log[l], dt_bias[l])
        o_a, s_new = gated_delta_chunked(q, k, v, g, beta, jnp.zeros((bp, H_A, DK_A, DV_A), F32))
        y_a = delta_out(o_a, z, delta_norm_w[l], w_proj_a[l])
        qr = partial_rope(qb.reshape(bp, sp, H_B, HD_B), pos_p)
        kr = partial_rope(kb.reshape(bp, sp, H_B, HD_B), pos_p)
        vr = vb.reshape(bp, sp, H_B, HD_B)
        y_b = moba_prompt(qr, kr, vr).astype(hp.dtype) @ w_proj_b[l]
        hp = merge_and_mlp(hp, y_a, y_b, ga, gb, w_out[l], norm2_w[l], w_up[l], w_down[l])
        kp_l.append(kr.astype(cache_k.dtype))
        vp_l.append(vr.astype(cache_v.dtype))
        dp_l.append(s_new.astype(state_delta.dtype))
        cp_l.append(conv_new.astype(state_conv.dtype))
        qkv, z, b_lg, a_lg, qb, kb, vb, ga, gb = in_proj(hs, norm1_w[l], w_in[l])
        q, k, v, g, beta, conv_new = delta_prep(qkv, state_conv[l], b_lg, a_lg,
                                                conv_w[l], a_log[l], dt_bias[l])
        o_a, s_new = gated_delta_recurrent(q, k, v, g, beta, state_delta[l].astype(F32))
        y_a = delta_out(o_a, z, delta_norm_w[l], w_proj_a[l])
        qr = partial_rope(qb.reshape(bs, ss, H_B, HD_B), pos_s)
        kr = partial_rope(kb.reshape(bs, ss, H_B, HD_B), pos_s)
        vr = vb.reshape(bs, ss, H_B, HD_B)
        y_b = moba_sample(qr, kr, vr, cache_k, cache_v, page_table, l).astype(hs.dtype) @ w_proj_b[l]
        hs = merge_and_mlp(hs, y_a, y_b, ga, gb, w_out[l], norm2_w[l], w_up[l], w_down[l])
        ks_l.append(kr.astype(cache_k.dtype))
        vs_l.append(vr.astype(cache_v.dtype))
        ds_l.append(s_new.astype(state_delta.dtype))
        cs_l.append(conv_new.astype(state_conv.dtype))
    y_prompt = rmsnorm(hp, norm_f_w)
    y_sample = rmsnorm(hs, norm_f_w)
    k_prompt = jnp.stack(kp_l)
    v_prompt = jnp.stack(vp_l)
    state_delta_prompt = jnp.stack(dp_l)
    state_conv_prompt = jnp.stack(cp_l)
    k_sample = jnp.stack(ks_l)
    v_sample = jnp.stack(vs_l)
    state_delta_sample = jnp.stack(ds_l)
    state_conv_sample = jnp.stack(cs_l)
    return (y_prompt, y_sample, k_prompt, v_prompt, state_delta_prompt, state_conv_prompt,
            k_sample, v_sample, state_delta_sample, state_conv_sample)


_drawn_inputs = setup_inputs


def setup_inputs(seed=0):
    import zlib

    import numpy as np

    out = dict(_drawn_inputs(seed))
    spreads = {}
    factors = {'delta_norm_w': 65.478,
     'norm2_w': 9.353,
     'norm_f_w': 23.397,
     'cache_k': 4.447,
     'cache_v': 4.073}
    for name, (base, spread) in spreads.items():
        noise = np.random.default_rng([zlib.crc32(name.encode()), seed]).standard_normal(out[name].shape)
        drawn = base * np.exp(spread * noise) if base else spread * noise
        out[name] = jnp.asarray(drawn.astype(out[name].dtype))
    for name, factor in factors.items():
        out[name] = (out[name] * factor).astype(out[name].dtype)
    return out
```

```python
from contextlib import ExitStack

import numpy as np
import concourse.bass as bass
from concourse import mybir

ALU = mybir.AluOpType
ACT = mybir.ActivationFunctionType
AX = mybir.AxisListType
F32 = mybir.dt.float32
F32R = mybir.dt.float32r
I32 = mybir.dt.int32
U8 = mybir.dt.uint8

P = 128
DM = 1024
SEQ = 512
NS = 8
NT = SEQ + NS
KT = DM // P
PAST = 2048
PAGE = 128
NPAGE = PAST // PAGE
HA, DA = 4, 128
CC = 3 * HA * DA
CW = 4
HB, DB = 8, 64
WB = HB * DB
NBLK = 8
TOPK = 3
ROT = DB // 4
HALF = ROT // 2
DFF = 4 * DM
EPS = 1e-6
BIG = 1e30
CHUNK = 128
NCH = SEQ // CHUNK
ATT_SCALE = DB ** -0.5
Q_SCALE = DA ** -0.5

C_Z, C_BA, C_Q, C_K, C_V, C_GA, C_GB = 1536, 2048, 2056, 2568, 3080, 3592, 4616

UNITS1 = ([("q", j, C_Q + P * j) for j in range(4)] + [("ba", 0, C_BA)]
          + [("k", j, C_K + P * j) for j in range(4)] + [("v", j, C_V + P * j) for j in range(4)]
          + [("c", j, P * j) for j in range(12)] + [("z", j, C_Z + P * j) for j in range(4)])
N1 = len(UNITS1)
U_GATE = N1
U_MERGE = U_GATE + 16
U_OUT = U_MERGE + 8
U_MLP = U_OUT + 8
NU = U_MLP + 64

K_ID, K_ONE, K_TRI, K_CAUS, K_STRICT, K_INCT, K_LT8, K_ROPE = 0, 128, 256, 384, 512, 640, 768, 832
K_N = K_ROPE + 5 * ROT
LEVELS = 7

GROUPS = NS * NPAGE // 2
RED_STEP0 = 6
RED_T1 = 2 * (N1 - RED_STEP0)

R_N1, R_N2, R_CW, R_DN, R_N = 0, 8, 16, 64, 65


def constants():
    i = np.arange(P)
    c = np.zeros((P, K_N), np.float32)
    c[:, K_ID:K_ID + P] = np.eye(P)
    c[:, K_ONE:K_ONE + P] = 1.0
    c[:, K_TRI:K_TRI + P] = i[:, None] <= i[None, :]
    c[:, K_CAUS:K_CAUS + P] = np.where(i[None, :] <= i[:, None], 0.0, -BIG)
    c[:, K_STRICT:K_STRICT + P] = np.where(i[None, :] < i[:, None], 0.0, -BIG)
    c[:, K_INCT:K_INCT + P] = np.where(i[:, None] <= i[None, :], 0.0, -BIG)
    n = np.arange(8)
    c[:, K_LT8:K_LT8 + 64] = (n[None, :] < n[:, None]).reshape(1, 64)
    inv = np.exp(np.arange(HALF, dtype=np.float32) * np.float32(-2.0 * np.log(500000.0) / ROT))
    pos = np.full((5, P), PAST, np.float32)
    pos[:4] = np.arange(SEQ).reshape(4, P)
    ang = pos.T[:, :, None] * inv
    c[:, K_ROPE:] = np.concatenate([np.cos(ang), np.sin(ang)], -1).reshape(P, 5 * ROT)
    m = np.zeros((P, 2, LEVELS, P), np.float32)
    for lv in range(LEVELS):
        s = 1 << lv
        low = ((i[:, None] // s) % 2 == 1) & (i[None, :] // s == i[:, None] // s - 1)
        m[:, 0, lv] = low
        m[:, 1, lv] = low.T
    return c, m.reshape(P, 2 * LEVELS * P)


class Link:

    def __init__(self, eng, sem):
        self.eng, self.sem, self.n = eng, sem, 0

    def __call__(self, ins):
        self.n = self.n + 1
        ins.then_inc(self.sem, 1)
        self.eng.wait_ge(self.sem, self.n)


def hybrid_step(nc, const_f, const_m, x_prompt, x_sample, cache_k, cache_v, page_table, state_delta, state_conv,
                norm1_w, w_in, conv_w, a_log, dt_bias, delta_norm_w, w_proj_a, w_proj_b, w_out, norm2_w,
                w_up, w_down, norm_f_w, y_prompt, y_sample, k_prompt, v_prompt, sd_prompt, sc_prompt,
                k_sample, v_sample, sd_sample, sc_sample):
    ht_dram = nc.dram_tensor("ht_dram", [P, KT, NT], F32, kind="Internal").ap()
    xp, xs = x_prompt[0], x_sample.rearrange("b s d -> (b s) d")
    ck = cache_k[0].rearrange("n l h d -> n l (h d)")
    cv = cache_v[0].rearrange("n l h d -> n l (h d)")

    with ExitStack() as ctx:
        pos = [16512]

        def at(name, shape, dt=F32, offset=None):
            size = int(np.prod(shape[1:])) * (1 if dt == U8 else 4)
            if offset is None:
                offset = pos[0]
                pos[0] += (size + 31) // 32 * 32
            return nc.alloc_sbuf_tensor_at(name, shape, dt, offset=offset)

        w_raw = at("w_raw", [P, 4, KT, P])
        split_at = pos[0]
        w_high = at("w_high", [P, 2, KT, P], F32R)
        w_low = at("w_low", [P, 2, KT, P], F32R)
        prob = at("prob", [P, 2, 512], F32, split_at)
        sq_ = at("sqb", [P, 2, HA, DA], F32, split_at)
        probt = at("probt", [P, 2, 512], F32, split_at + 8192)
        xh = at("xh", [P, KT, NT], F32R)
        xl = at("xl", [P, KT, NT], F32R)
        ht_at = pos[0]
        ht = at("ht", [P, KT, NT])
        gate_a = at("gate_a", [P, 8, NT], F32, ht_at)
        cf = at("cf", [P, K_N])
        cm = at("cm", [P, 2, LEVELS, P], U8)
        fw = at("fw", [P, R_N])
        pt = at("pt", [1, P], I32)
        alog = at("alog", [P, HA])
        dtb = at("dtb", [P, HA])
        ss = at("ss", [P, 8])
        rstd = at("rstd", [P, 8])
        ba = at("ba", [P, 5, 8])
        beta = at("beta", [P, 5, HA])
        nbeta = at("nbeta", [P, 5, HA])
        gg = at("gg", [P, 5, HA])
        gt = at("gt", [P, 5, HA])
        gc = at("gc", [P, NCH, HA])
        egc = at("egc", [P, NCH, HA])
        glx = at("glx", [P, NCH, 2 * HA])
        ckb = at("ckb", [P, NCH, HA])
        qks = at("qks", [P, NCH, 2 * HA])
        tail = at("tail", [P, 12, 3 + NS])
        xp4 = at("xp4", [P, 12, NS, CW])
        cvs = at("cvs", [P, 12, NS])
        vnew_s = at("vnew_s", [P, 4, NS])
        smx = at("smx", [P, 2])
        nbias = at("nbias", [P, 2])
        rs = at("rs", [P, 4 * HB])
        rrs = at("rrs", [P, HB])
        own = at("own", [NS, HB])
        s1 = at("s1", [P, 64])
        s2 = at("s2", [P, 64])
        s3 = at("s3", [P, 64])
        s4 = at("s4", [P, 64])
        s5 = at("s5", [P, 32])
        s6 = at("s6", [P, 32])
        on_st = at("on_st", [P, HA])
        rb = at("rb", [P, NT])

        r2 = pos[0]
        ona_h = at("ona_h", [P, 4, NT], F32R)
        ona_l = at("ona_l", [P, 4, NT], F32R)
        onb_h = at("onb_h", [P, 4, NT], F32R)
        onb_l = at("onb_l", [P, 4, NT], F32R)
        qb = at("qb", [P, NS, WB], F32, r2)
        gcmp = at("gcmp", [NS, 512], F32, r2)
        ecmp = at("ecmp", [NS, 512], F32, r2 + 2048)
        bd8 = at("bd8", [NS, NS, P], F32, r2 + 4096)
        pmt = at("pmt", [NS, 2, P], F32, r2 + 8192)
        sel = at("sel", [NS, 64], F32, r2 + 9216)
        blk = at("blk", [NS, 2, 64], F32, r2 + 9472)
        cst = at("cst", [3 + NS, CC], F32, r2 + 10240)
        mtqk = at("mtqk", [P, 4, 2 * WB], F32, r2 + 16640)
        junk = at("junk", [P, DM], F32, r2 + 16640)
        xn = at("xn", [P, 2, NT], F32, r2 + 16640 + 4096)

        r1 = pos[0]
        ring = at("ring", [P, 4, 2, WB], F32, r1)
        lg = at("lg", [P, NS, HB, NPAGE], F32, r1 + 16384)
        mtv = at("mtv", [P, 4, WB], F32, r1 + 20480)
        cmf = at("cmf", [P, 2, LEVELS, P], F32, r1 + 20480)
        vnew = at("vnew", [P, HA, DA], F32, r1 + 20480)
        st = at("st", [P, 2, HA, DA], F32, r1 + 22528)
        tm = at("tm", [P, NCH, CC], F32, r1 + 28672)
        xin = at("xin", [P, 5, DM], F32, r1 + 28672)
        wr = at("wr", [R_N, P], F32, r1 + 28672 + 20480)
        state = at("state", [P, NS * HA, DA], F32, r1 + 36864)
        zs = at("zs", [P, 4, NT], F32, r1 + 53248)
        mts = at("mts", [NS, 3 * WB], F32, r1 + 61568)
        mq = at("mq", [P, 2, NT], F32, r1 + 67712)
        pre = at("pre", [P, 2, 3 + SEQ], F32, r1 + 71872)
        cvr = at("cvr", [P, 2, SEQ], F32, r1 + 76000)
        scr = at("scr", [3 * NS, CC], F32, r1 + 71872)
        baf = at("baf", [8, NT], F32, r1 + 80128)
        qt = at("qt", [P, 4, SEQ], F32, r1 + 61568)
        kt = at("kt", [P, 4, SEQ], F32, r1 + 69760)
        ob = at("ob", [P, WB], F32, r1 + 77952)
        d0 = r1 + 61568
        qgt = at("qgt", [P, 2, HA, P], F32, d0)
        Dm = at("Dm", [P, 2, HA, P], F32, d0 + 4096)
        Em = at("Em", [P, 2, HA, P], F32, d0 + 8192)
        An = at("An", [P, 2, HA, P], F32, d0 + 12288)
        qkt = at("qkt", [P, 2, HA, P], F32, d0 + 16384)
        bd = at("bd", [32, 32, DA], F32, d0)
        dlt = at("dlt", [32, DA], F32, d0 + 16384)
        knt = at("knt", [32, DA], F32, d0 + 16896)
        sq4 = at("sq4", [P, NCH, 2 * HA, DA], F32, d0)
        gate_b = at("gate_b", [P, 8, NT], F32, r1)
        mh = at("mh", [P, KT, NT], F32R, r1)
        ml = at("ml", [P, KT, NT], F32R, r1 + 16640)
        sga = at("sga", [P, NT], F32, r1 + 53248)
        sgb = at("sgb", [P, NT], F32, r1 + 55328)
        mx_ = at("mx_", [P, NT], F32, r1 + 57408)
        sqh = at("sqh", [P, 2, NT], F32, r1 + 33280)
        ssum = at("ssum", [P, NT], F32, r1 + 37440)
        rel = at("rel", [P, 2, NT], F32, r1 + 39520)
        uu = at("uu", [P, 2, NT], F32, r1 + 43680)
        wf = at("wf", [P, DM], F32, r1 + 61568)
        yy = at("yy", [P, 2, DM], F32, r1 + 65664)
        assert r1 + 82208 <= 229376, r1 + 82208

        ps = ctx.enter_context(nc.psum_tensor("ps", [P, 8 * 512], F32))

        def bank(b, n=512, rows=P):
            return ps[0:rows, b * 512:b * 512 + n]

        def unit_ps(b):
            return ps[:, b * 1024 + 256:b * 1024 + 256 + NT]

        ident, ones = cf[:, K_ID:K_ID + P], cf[:, K_ONE:K_ONE + P]

        def sem(name):
            return ctx.enter_context(nc.semaphore(name))

        def bc(ap, shape):
            return ap.broadcast_to(shape)

        (c_landed, x_landed0, x_landed1, x_landed2, x_landed3, x_landed4, pt_landed, st_landed, stored, stored_kv,
         stored_cs, wf_landed, ht_kept, ht_landed) = [sem(n) for n in (
            "c_landed", "x_landed0", "x_landed1", "x_landed2", "x_landed3", "x_landed4", "pt_landed", "st_landed",
            "stored", "stored_kv", "stored_cs", "wf_landed", "ht_kept", "ht_landed")]
        x_landed = [x_landed0, x_landed1, x_landed2, x_landed3, x_landed4]
        w_landed = [sem(f"w_landed{i}") for i in range(4)]
        kv_landed = [sem(f"kv_landed{i}") for i in range(4)]
        a_own, v_own, g_own = sem("a_own"), sem("v_own"), sem("g_own")
        w_split_hi, w_split_lo, unit_done = sem("w_split_hi"), sem("w_split_lo"), sem("unit_done")
        unit_out = sem("unit_out")
        names = """x_squares ms_ready xt_turned ht_out xn_ready xh_out xl_out mq_turned mt_out mts_out vn_out qb_sums qb_out rope_k
            k_prod k_red conv_out silu_out tm_turned tm_out qk_turned qk_out att_sums att_max att_exp pt_turned
            pt_out att_pv ob_out ob_turned onb_h_out onb_l_out sel_turned pv_done sq_out sq_red gu_ready gb_sums
            dec_in dec_n dec_t gl_in gl_out q_scaled qg_scaled k_scaled k_ready q_turned qt_out qg_turned
            qgt_out ktr_turned kt_out kk_sums an_ready qk_sums qkt_ready d_ready e_turned e_out lv_q lv_q_out
            lv_e lv_e_out lv_d lv_d_out wt_sums wt_out vn_sums vn_new o_sums s_sums s_out osq_out on_ms on_root
            on_ready on_turned on_gated ona_h_out ona_l_out sm_t1 sm_outer sm_outer_out gate_out mix_ready
            mh_out ml_out h_out sq2_out ssum_ready hx_h hx_l rel_out relsq_out uu_ready uh_out ul_out yt_turned
            y_sq y_ms y_root y_out""".split()
        S = {n: sem(n) for n in names}

        once = {
            "vector": """rstd_ready fw_out scr_out masks_out pre_zero rope_q ba_out own_out sp_in gate_ready sel_red bias_ready
                lg_biased row_sums den_out gc_out ssr_in sm_conv sm_ms sm_bd sm_decay sm_dlt sm_bdo
                sm_oms sm_on os_ready os_l inv_ready""".split(),
            "scalar": """root_ready rb_out sig_out sp_out tail_out lg_exp own_exp egc_out ssr_out sm_silu sm_root sm_bdin
                sm_t1o sm_osq sm_oroot sm_oh os_h""".split(),
            "tensor": """fw_turned rb_sums scr_turned ba_turned tail_turned sel2_turned bias_sums den_sums gc_sums sm_sums
                sm_bsums sm_kv sm_o sm_osum ss_sums""".split(),
        }
        once_sem = {engine: sem(f"{engine}_steps") for engine in once}
        once_at = {name: (engine, i) for engine, steps in once.items() for i, name in enumerate(steps)}
        once_done = dict.fromkeys(once, 0)

        def did(name):
            engine, i = once_at[name]
            assert once_done[engine] == i, name
            once_done[engine] += 1
            return once_sem[engine], 1

        def done(name):
            engine, i = once_at[name]
            return once_sem[engine], i + 1

        def w_source(u):
            def cut(w, row, col):
                return w[row:row + 512, col:col + P].rearrange("(k p) m -> p k m", p=P)
            if u < N1:
                c = UNITS1[u][2]
                return cut(w_in[0], 0, c), cut(w_in[0], 512, c)
            if u < U_MERGE:
                branch, j = divmod(u - U_GATE, 8)
                c = (C_GA, C_GB)[branch] + P * j
                return cut(w_in[0], 0, c), cut(w_in[0], 512, c)
            if u < U_OUT:
                j = u - U_MERGE
                return cut(w_proj_a[0], 0, P * j), cut(w_proj_b[0], 0, P * j)
            j = u - U_OUT
            return cut(w_out[0], 0, P * j), cut(w_out[0], 512, P * j)

        def load_unit(eng, u):
            if u >= 4:
                eng.wait_ge(S_lo, u - 3)
            for half, src in enumerate(w_source(u)):
                eng.dma_start(w_raw[:, u % 4, 4 * half:4 * half + 4, :], src).then_inc(w_landed[u % 4], 16)

        S_hi, S_lo = w_split_hi, w_split_lo

        def split_high(act, u, base=0):
            s = u % 4
            act.wait_ge(w_landed[s], 32 * (u // 4 + 1) + base * 8)
            if not isinstance(base, int) or base + u >= 2:
                act.wait_ge(unit_done, base + (u - 1))
            act.activation(w_high[:, u % 2], w_raw[:, s], ACT.Copy).then_inc(S_hi, 1)

        def split_low(dve, u, base=0):
            dve.wait_ge(S_hi, base + (u + 1))
            dve.tensor_tensor(w_low[:, u % 2], w_raw[:, u % 4], w_high[:, u % 2].bitcast(F32),
                              ALU.subtract).then_inc(S_lo, 1)

        def product(pe, u, out, rhs_h, rhs_l, ks=range(KT), slot=None, before_k=None):
            n, last = len(ks), None
            for i, k in enumerate(ks):
                if before_k is not None:
                    before_k(i)
                for w, x in ((w_high, rhs_h), (w_high, rhs_l), (w_low, rhs_h)):
                    for a, b in ((0, 256), (256, NT)):
                        last = pe.matmul(out[:, a:b], w[:, u % 2, k, :], x[:, i, a:b],
                                         start=(i == 0 and w is w_high and x is rhs_h),
                                         stop=(i == n - 1 and w is w_low), skip_group_check=True)
            return last

        block = ctx.enter_context(nc.Block())

        @block.sync
        def _(sp):
            for t in range(4):
                sp.dma_start(xin[:, t, :], xp[t * P:(t + 1) * P, :]).then_inc(x_landed[t], 16)
            sp.dma_start(xin[0:NS, 4, :], xs).then_inc(x_landed[4], 16)
            sp.dma_start(cf[:], const_f).then_inc(c_landed, 16)
            sp.dma_start(wr[R_N1:R_N1 + 8, :], norm1_w[0].rearrange("(t p) -> t p", p=P)).then_inc(c_landed, 16)
            sp.dma_start(wr[R_N2:R_N2 + 8, :], norm2_w[0].rearrange("(t p) -> t p", p=P)).then_inc(c_landed, 16)
            sp.dma_start(wr[R_CW:R_CW + 48, :], conv_w[0].rearrange("i (t p) -> (i t) p", p=P)).then_inc(c_landed, 16)
            sp.dma_start(wr[R_DN:R_DN + 1, :], delta_norm_w).then_inc(c_landed, 16)
            sp.dma_start(cmf[:], const_m.rearrange("p (a l c) -> p a l c", a=2, l=LEVELS)).then_inc(c_landed, 16)
            sp.dma_start(alog[:], bc(a_log, [P, HA])).then_inc(c_landed, 16)
            sp.dma_start(dtb[:], bc(dt_bias, [P, HA])).then_inc(c_landed, 16)
            sp.dma_start(scr[:], state_conv[0].rearrange("b i c -> (b i) c")).then_inc(c_landed, 16)
            sp.dma_start(pt[:], page_table.rearrange("b n -> (b n)").rearrange("(o n) -> o n", o=1)).then_inc(pt_landed, 16)
            sp.dma_start(sc_sample[0, :, 0:2, :], state_conv[0, :, 1:3, :]).then_inc(stored, 16)
            sp.wait_ge(pt_landed, 16)
            npool = cache_k.shape[1]

            def stream(cache, first, free, base):
                for r in range(8):
                    if r >= 4 or not first:
                        sp.wait_ge(free, base + (r - 3))
                    for i in range(2):
                        page = sp.value_load(pt[0:1, bass.ds(base * 2 + (2 * r + i), 1)], min_val=0, max_val=npool - 1)
                        sp.dma_start(ring[:, r % 4, i, :],
                                     cache[bass.ds(page, 1), :, :].rearrange("o l c -> l (o c)"))\
                            .then_inc(kv_landed[r % 4], 16)

            stream(ck, True, S["k_red"], 0)
            with sp.Fori(1, NS) as b:
                stream(ck, False, S["k_red"], b * 8)
            for r in range(8):
                if r < 4:
                    sp.wait_ge(S["k_red"], GROUPS - 3 + r)
                else:
                    sp.wait_ge(S["pv_done"], r - 3)
                for i in range(2):
                    page = sp.value_load(pt[0:1, 2 * r + i:2 * r + i + 1], min_val=0, max_val=npool - 1)
                    sp.dma_start(ring[:, r % 4, i, :], cv[bass.ds(page, 1), :, :].rearrange("o l c -> l (o c)"))\
                        .then_inc(kv_landed[r % 4], 16)
            with sp.Fori(1, NS) as b:
                stream(cv, False, S["pv_done"], b * 8)
            for u in range(U_GATE + 12, U_MLP):
                load_unit(sp, u)
                if u == U_GATE + 12:
                    sp.wait_ge(S["s_out"], NCH)
                    sp.dma_start(sd_prompt[0, 0].rearrange("h d e -> d h e"), st[:, NCH % 2]).then_inc(stored, 16)
                if u == U_MERGE + 4:
                    sp.wait_ge(S["sm_outer_out"], 8)
                    sp.dma_start(sd_sample[0].rearrange("b h d e -> d (b h) e"), state[:]).then_inc(stored, 16)
                if u >= U_OUT:
                    j = u - U_OUT
                    sp.wait_ge(S["mix_ready"], j + 1)
                    sp.dma_start(ht[:, j], ht_dram[:, j]).then_inc(ht_landed, 16)
            with sp.Fori(0, 4) as g:
                for i in range(16):
                    sp.wait_ge(S_lo, g * 16 + (U_MLP + i - 3))
                    for half in range(2):
                        if i < 8:
                            src = w_up[0][512 * half:512 * half + 512, bass.ds(g * 1024 + i * P, P)]
                        else:
                            src = w_down[0][bass.ds(g * 1024 + 512 * half, 512), (i - 8) * P:(i - 7) * P]
                        sp.dma_start(w_raw[:, (U_MLP + i) % 4, 4 * half:4 * half + 4, :],
                                     src.rearrange("(k p) m -> p k m", p=P)).then_inc(w_landed[(U_MLP + i) % 4], 16)
            sp.wait_ge(S["ona_h_out"], NCH)
            sp.dma_start(wf[:], bc(norm_f_w.rearrange("(o n) -> o n", o=1), [P, DM])).then_inc(wf_landed, 16)
            for t in range(5):
                sp.wait_ge(S["y_out"], t + 1)
                if t < 4:
                    sp.dma_start(y_prompt[0, t * P:(t + 1) * P, :], yy[:, t % 2]).then_inc(stored, 16)
                else:
                    sp.dma_start(y_sample.rearrange("b s d -> (b s) d"), yy[0:NS, 0]).then_inc(stored, 16)
                if t < 3:
                    sp.wait_ge(stored, 16 * (4 + t))
            sp.wait_ge(stored, 16 * 8)
            sp.wait_ge(stored_kv, 16 * 4)
            sp.wait_ge(stored_cs, 16 * 2)

        @block.gpsimd
        def _(g):
            g.wait_ge(S["qb_out"], NS)
            for b in range(NS):
                for r in range(8):
                    g.wait_ge(kv_landed[r % 4], b * 64 + 32 * (r // 4 + 1))
                    g.tensor_tensor(ring[:, r % 4], ring[:, r % 4], bc(qb[:, b:b + 1, :], [P, 2, WB]), ALU.mult)\
                        .then_inc(S["k_prod"], 1)

        @block.scalar
        def _(act):
            A = act.activation
            link = Link(act, a_own)
            for u in range(4):
                load_unit(act, u)
            for t in range(5):
                n = P if t < 4 else NS
                act.wait_ge(x_landed[t], 16)
                if t == 0:
                    act.wait_ge(S["ms_ready"], 1)
                A(junk[0:n, :], xin[0:n, t, :], ACT.Square, accum_out=ss[0:n, t:t + 1]).then_inc(S["x_squares"], 1)
                act.wait_ge(S["x_squares"], t + 1)
            act.wait_ge(S["ms_ready"], 2)
            A(rstd[:], ss[:], ACT.Sqrt).then_inc(*did("root_ready"))
            split_high(act, 0)
            split_high(act, 1)
            act.wait_ge(*done("rb_sums"))
            A(rb[:], unit_ps(3), ACT.Copy).then_inc(*did("rb_out"))
            for k in range(KT + 1):
                if k < KT:
                    act.wait_ge(S["xt_turned"], k + 1)
                    A(ht[:, k], unit_ps(k % 3), ACT.Copy).then_inc(S["ht_out"], 1)
                if k > 0:
                    act.wait_ge(S["xn_ready"], k)
                    A(xh[:, k - 1], xn[:, (k - 1) % 2], ACT.Copy).then_inc(S["xh_out"], 1)
            load_unit(act, 4)
            act.wait_ge(S["ht_out"], KT)
            act.dma_start(ht_dram, ht[:]).then_inc(ht_kept, 16)

            def turned_out(m):
                act.wait_ge(S["mq_turned"], m + 1)
                if m == 8:
                    act.wait_ge(*done("masks_out"))
                src = bank(4 + m % 2).rearrange("p (t c) -> p t c", t=4)
                dst = mtqk[:, :, m * P:(m + 1) * P] if m < 8 else mtv[:, :, (m - 8) * P:(m - 7) * P]
                A(dst, src, ACT.Copy).then_inc(S["mt_out"], 1)

            def conv_turned_out(j):
                act.wait_ge(S["tm_turned"], j + 1)
                A(tm[:, :, j * P:(j + 1) * P], bank(4 + j % 2).rearrange("p (t c) -> p t c", t=4), ACT.Copy)\
                    .then_inc(S["tm_out"], 1)

            def silu(j):
                act.wait_ge(S["conv_out"], j + 1)
                A(cvr[:, j % 2], cvr[:, j % 2], ACT.Silu).then_inc(S["silu_out"], 1)

            m_of = {u: (j if kind == "q" else 4 + j if kind == "k" else 8 + j)
                    for u, (kind, j, _) in enumerate(UNITS1) if kind in "qkv"}
            for u, (kind, j, _) in enumerate(UNITS1):
                if u + 5 < U_GATE + 4:
                    load_unit(act, u + 5)
                if u + 2 <= U_GATE:
                    split_high(act, u + 2)
                act.wait_ge(unit_done, u + 1)
                if kind in "qkv":
                    m = m_of[u]
                    if m >= 2:
                        act.wait_ge(S["mq_turned"], m - 1)
                    A(mq[:, m % 2], unit_ps(u % 2), ACT.Copy).then_inc(unit_out, 1)
                    if kind == "v":
                        act.wait_ge(unit_out, u + 1)
                        A(vnew_s[:, j], mq[:, m % 2, SEQ:NT], ACT.Copy).then_inc(S["vn_out"], 1)
                        act.wait_ge(S["vn_out"], j + 1)
                elif kind == "ba":
                    A(baf[:], unit_ps(u % 2)[0:8, :], ACT.Copy).then_inc(unit_out, 1)
                elif kind == "c":
                    if j == 0:
                        act.wait_ge(*done("scr_out"))
                        act.wait_ge(*done("pre_zero"))
                    if j >= 2:
                        act.wait_ge(S["conv_out"], j - 1)
                    link(A(pre[:, j % 2, 3:3 + SEQ], unit_ps(u % 2)[:, 0:SEQ], ACT.Copy))
                    A(tail[:, j], unit_ps(u % 2)[:, SEQ - 3:NT], ACT.Copy).then_inc(unit_out, 1)
                    if j >= 1:
                        silu(j - 1)
                    if j >= 2:
                        conv_turned_out(j - 2)
                else:
                    A(zs[:, j], unit_ps(u % 2), ACT.Silu).then_inc(unit_out, 1)
                    if j == 0:
                        silu(11)
                        conv_turned_out(10)
                    if j == 1:
                        conv_turned_out(11)
                if u in (5, 6):
                    for b in range(4 * (u - 5), 4 * (u - 5) + 4):
                        act.wait_ge(S["qb_sums"], b + 1)
                        A(qb[:, b], bank(4 + b % 4), ACT.Copy).then_inc(S["qb_out"], 1)
                if u - 1 in m_of:
                    turned_out(m_of[u - 1])
                if u == 11:
                    act.wait_ge(S["rope_k"], 2)
                    act.dma_start(k_prompt[0, 0].rearrange("(t p) h d -> p t (h d)", p=P), mtqk[:, :, WB:])\
                        .then_inc(stored_kv, 16)
                    act.dma_start(k_sample[0].rearrange("b s h d -> (b s) (h d)"), mts[:, WB:2 * WB])\
                        .then_inc(stored_kv, 16)
                if u == 15:
                    act.wait_ge(S["mt_out"], 12)
                    act.wait_ge(S["mts_out"], 12)
                    act.dma_start(v_prompt[0, 0].rearrange("(t p) h d -> p t (h d)", p=P), mtv[:])\
                        .then_inc(stored_kv, 16)
                    act.dma_start(v_sample[0].rearrange("b s h d -> (b s) (h d)"), mts[:, 2 * WB:])\
                        .then_inc(stored_kv, 16)

            A(beta[:], ba[:, :, 0:HA], ACT.Sigmoid).then_inc(*did("sig_out"))
            link(A(alog[:], alog[:], ACT.Exp))
            act.wait_ge(*done("sp_in"))
            link(A(gt[:], gt[:], ACT.Exp, scale=-1.0))
            A(gt[:], gt[:], ACT.Ln, bias=1.0).then_inc(*did("sp_out"))

            act.wait_ge(stored_kv, 64)
            act.wait_ge(*done("own_out"))
            for n in range(8):
                act.wait_ge(S["qk_turned"], n + 1)
                if n == 0:
                    act.wait_ge(S["conv_out"], 12)
                    act.wait_ge(*done("ba_out"))
                A((qt if n < 4 else kt)[:, n % 4], bank(n % 4), ACT.Copy).then_inc(S["qk_out"], 1)

            for n in range(4 * HB):
                q_t, h = divmod(n, HB)
                N = (q_t + 1) * P
                act.wait_ge(S["att_max"], n + 1)
                if n >= 2:
                    act.wait_ge(S["pt_turned"], n - 1)
                A(prob[:, n % 2, 0:N], bank(n % 4, N), ACT.Exp, bias=nbias[:, n % 2:n % 2 + 1], scale=ATT_SCALE,
                  accum_out=rs[:, n:n + 1]).then_inc(S["att_exp"], 1)
                if n >= 1:
                    m = n - 1
                    act.wait_ge(S["pt_turned"], m + 1)
                    if m >= 2:
                        act.wait_ge(S["att_pv"], m - 1)
                    M = (m // HB + 1) * P
                    A(probt[:, m % 2, 0:M], bank(4 + m % 2, M), ACT.Copy).then_inc(S["pt_out"], 1)
                if h == 3 and q_t >= 1:
                    c = q_t - 1
                    act.wait_ge(S["ob_turned"], c + 1)
                    A(onb_h[:, :, c * P:(c + 1) * P], bank(6 + c % 2).rearrange("p (t c) -> p t c", t=4),
                      ACT.Copy).then_inc(S["onb_h_out"], 1)
            act.wait_ge(S["pt_turned"], 32)
            act.wait_ge(S["att_pv"], 30)
            A(probt[:, 1, :], bank(5), ACT.Copy).then_inc(S["pt_out"], 1)
            act.wait_ge(S["ob_turned"], 4)
            A(onb_h[:, :, 3 * P:4 * P], bank(7).rearrange("p (t c) -> p t c", t=4), ACT.Copy)\
                .then_inc(S["onb_h_out"], 1)

            def gate(n):
                u = U_GATE + n
                act.wait_ge(unit_done, u + 1)
                if n != 7:
                    split_high(act, u + 2)
                if n == 0:
                    act.wait_ge(ht_kept, 16)
                A((gate_a if n < 8 else gate_b)[:, n % 8], unit_ps(u % 2), ACT.Sigmoid).then_inc(S["gate_out"], 1)

            split_high(act, U_GATE + 1)
            act.wait_ge(*done("tail_turned"))
            act.wait_ge(S["k_prod"], GROUPS)
            A(cst[:], ps[0:3 + NS, 5 * 512:5 * 512 + CC], ACT.Copy).then_inc(*did("tail_out"))
            act.wait_ge(*done("tail_out"))
            act.dma_start(sc_prompt[0, 0], cst[0:3, :]).then_inc(stored_cs, 16)
            act.dma_start(sc_sample[0, :, 2, :], cst[3:3 + NS, :]).then_inc(stored_cs, 16)

            for n in range(4):
                if n < 3:
                    load_unit(act, U_GATE + 4 + n)
                gate(n)
            load_unit(act, U_GATE + 7)
            act.wait_ge(*done("lg_biased"))
            A(lg[:], lg[:], ACT.Exp, scale=ATT_SCALE).then_inc(*did("lg_exp"))
            A(own[:], own[:], ACT.Exp, scale=ATT_SCALE).then_inc(*did("own_exp"))
            for n in (4, 5):
                load_unit(act, U_GATE + 4 + n)
                gate(n)
            act.wait_ge(*done("gc_out"))
            A(egc[:], gc[:], ACT.Exp).then_inc(*did("egc_out"))
            for c in range(NCH):
                A(sq4[:, c].rearrange("p a d -> p (a d)"), tm[:, c, 0:2 * HA * DA], ACT.Square).then_inc(S["sq_out"], 1)
            for n in (6, 7):
                load_unit(act, U_GATE + 4 + n)
                gate(n)

            act.wait_ge(*done("ssr_in"))
            A(qks[:], qks[:], ACT.Sqrt).then_inc(*did("ssr_out"))

            for pair in range(NCH // 2):
                for p in range(2):
                    c = 2 * pair + p
                    act.wait_ge(S["dec_in"], 2 * c + 2)
                    A(An[:, p], An[:, p], ACT.Exp).then_inc(S["dec_n"], 1)
                    A(qkt[:, p], qkt[:, p], ACT.Exp).then_inc(S["dec_t"], 1)
                    act.wait_ge(S["gl_in"], c + 1)
                    A(glx[:, c], glx[:, c], ACT.Exp).then_inc(S["gl_out"], 1)
                for p in range(2):
                    c = 2 * pair + p
                    act.wait_ge(S["q_turned"], c + 1)
                    A(Dm[:, p], bank(4 + 2 * p).rearrange("p (h c) -> p h c", h=HA), ACT.Copy).then_inc(S["qt_out"], 1)
                    act.wait_ge(S["ktr_turned"], c + 1)
                    A(Em[:, p], bank(5 + 2 * p).rearrange("p (h c) -> p h c", h=HA), ACT.Copy).then_inc(S["kt_out"], 1)
                    act.wait_ge(S["qg_turned"], c + 1)
                    A(qgt[:, p], bank(p).rearrange("p (h c) -> p h c", h=HA), ACT.Copy).then_inc(S["qgt_out"], 1)
                for p in range(2):
                    c = 2 * pair + p
                    act.wait_ge(S["e_turned"], c + 1)
                    A(Em[:, p], bank(4 + 2 * p).rearrange("p (h c) -> p h c", h=HA), ACT.Copy).then_inc(S["e_out"], 1)
                for lv in range(1, LEVELS):
                    for p in range(2):
                        act.wait_ge(S["lv_q"], 2 * ((LEVELS - 1) * pair + lv - 1) + p + 1)
                        A(sq_[:, p], bank(p).rearrange("p (h c) -> p h c", h=HA), ACT.Copy).then_inc(S["lv_q_out"], 1)
                for p in range(2):
                    act.wait_ge(S["wt_sums"], 2 * pair + p + 1)
                    A(Dm[:, p], bank(p).rearrange("p (h c) -> p h c", h=HA), ACT.Copy).then_inc(S["wt_out"], 1)
                for p in range(2):
                    c = 2 * pair + p
                    act.wait_ge(S["vn_sums"], c + 1)
                    A(vnew[:], bank(4 + 2 * p).rearrange("p (h c) -> p h c", h=HA), ACT.Copy).then_inc(S["vn_new"], 1)
                    act.wait_ge(S["o_sums"], c + 1)
                    A(sq_[:, p], bank(5 + 2 * p).rearrange("p (h c) -> p h c", h=HA), ACT.Square)\
                        .then_inc(S["osq_out"], 1)
                    act.wait_ge(S["on_ms"], c + 1)
                    A(on_st[:], on_st[:], ACT.Sqrt).then_inc(S["on_root"], 1)
                    act.wait_ge(S["on_gated"], c + 1)
                    if c == 0:
                        act.wait_ge(stored_cs, 32)
                    A(ona_h[:, :, c * P:(c + 1) * P], An[:, p], ACT.Copy).then_inc(S["ona_h_out"], 1)

            act.wait_ge(S["ona_l_out"], NCH)
            act.dma_start(state[:], state_delta[0].rearrange("b h d e -> d (b h) e")).then_inc(st_landed, 16)
            act.wait_ge(S["on_turned"], NCH)
            split_high(act, U_GATE + 9)
            act.wait_ge(*done("sm_conv"))
            link(A(cvs[:], cvs[:], ACT.Silu))
            A(s1[:], cvs[:, 0:8, :].rearrange("p t b -> p (t b)"), ACT.Square).then_inc(*did("sm_silu"))
            gate(8)
            act.wait_ge(*done("sm_ms"))
            A(s1[:], s1[:], ACT.Sqrt).then_inc(*did("sm_root"))
            A(s5[0:NS, 0:HA], gg[0:NS, 4, :], ACT.Exp).then_inc(*did("sm_bdin"))
            for n in (9, 10, 11):
                gate(n)
            act.wait_ge(S["sm_t1"], 2)
            link(A(dlt[:], bank(4, DA, 32), ACT.Copy))
            A(knt[:], bank(5, DA, 32), ACT.Copy).then_inc(*did("sm_t1o"))
            gate(12)
            gate(13)
            act.wait_ge(*done("sm_o"))
            A(s1[:, 0:32], bank(4, 32), ACT.Square).then_inc(*did("sm_osq"))
            gate(14)
            act.wait_ge(*done("sm_oms"))
            A(s2[:, 0:32], s2[:, 0:32], ACT.Sqrt).then_inc(*did("sm_oroot"))
            act.wait_ge(*done("sm_on"))
            A(ona_h[:, :, SEQ:NT], s3[:, 0:32].rearrange("p (h b) -> p h b", h=HA), ACT.Copy).then_inc(*did("sm_oh"))
            act.wait_ge(*done("os_ready"))
            A(onb_h[:, :, SEQ:NT], s4[:, 0:32].rearrange("p (c b) -> p c b", c=4), ACT.Copy).then_inc(*did("os_h"))

            gate(15)

            for j in range(8):
                split_high(act, U_MERGE + j + 2)
                act.wait_ge(S["mix_ready"], j + 1)
                A(mh[:, j], mx_[:], ACT.Copy).then_inc(S["mh_out"], 1)

            for j in range(8):
                split_high(act, U_OUT + j + 2)
                act.wait_ge(S["h_out"], j + 1)
                if j >= 2:
                    act.wait_ge(S["ssum_ready"], j - 1)
                A(sqh[:, j % 2], ht[:, j], ACT.Square).then_inc(S["sq2_out"], 1)
                A(xh[:, j], ht[:, j], ACT.Copy, scale=fw[:, R_N2 + j:R_N2 + j + 1]).then_inc(S["hx_h"], 1)

            def mlp(g, last=False):
                for i in range(16):
                    if 1 <= i <= 8:
                        act.wait_ge(S["uu_ready"], g * 8 + i)
                        A(mh[:, i - 1], uu[:, (i - 1) % 2], ACT.Copy).then_inc(S["uh_out"], 1)
                    if not (last and i >= 14):
                        split_high(act, U_MLP + i + 2, g * 16)
                    if i < 8:
                        act.wait_ge(unit_done, g * 16 + (U_MLP + i + 1))
                        A(rel[:, i % 2], unit_ps((U_MLP + i) % 2), ACT.Relu).then_inc(S["rel_out"], 1)
                        act.wait_ge(S["rel_out"], g * 8 + (i + 1))
                        A(rel[:, i % 2], rel[:, i % 2], ACT.Square).then_inc(S["relsq_out"], 1)
            with act.Fori(0, 3) as g:
                mlp(g)
            mlp(3, True)

            for t in range(5):
                n = P if t < 4 else NS
                act.wait_ge(S["yt_turned"], t + 1)
                A(rel[:].rearrange("p a n -> p (a n)")[0:n, 0:DM], ps[0:n, (t % 4) * 1024:(t % 4) * 1024 + DM],
                  ACT.Square, accum_out=ss[0:n, t:t + 1]).then_inc(S["y_sq"], 1)
                act.wait_ge(S["y_ms"], t + 1)
                A(rstd[0:n, t:t + 1], ss[0:n, t:t + 1], ACT.Sqrt).then_inc(S["y_root"], 1)

        @block.vector
        def _(v):
            link = Link(v, v_own)
            TT, TS, STT = v.tensor_tensor, v.tensor_scalar, v.scalar_tensor_tensor

            link(v.memset(ba[:], 0.0))
            v.memset(ss[:], 1.0).then_inc(S["ms_ready"], 1)
            v.wait_ge(S["ms_ready"], 1)
            v.wait_ge(S["x_squares"], 5)
            TS(ss[:], ss[:], 1.0 / DM, EPS, ALU.mult, ALU.add).then_inc(S["ms_ready"], 1)
            v.wait_ge(*done("root_ready"))
            v.reciprocal(rstd[:], rstd[:]).then_inc(*did("rstd_ready"))
            v.wait_ge(*done("fw_turned"))
            v.tensor_copy(fw[:], ps[:, 1024:1024 + R_N]).then_inc(*did("fw_out"))
            v.wait_ge(*done("fw_out"))
            v.wait_ge(*done("rb_out"))
            for k in range(KT + 1):
                if k < KT:
                    v.wait_ge(S["ht_out"], k + 1)
                    if k >= 2:
                        v.wait_ge(S["xl_out"], k - 1)
                        v.wait_ge(S["xh_out"], k - 1)
                    STT(xn[:, k % 2], ht[:, k], fw[:, R_N1 + k:R_N1 + k + 1], rb[:], ALU.mult, ALU.mult)\
                        .then_inc(S["xn_ready"], 1)
                if k > 0:
                    v.wait_ge(S["xh_out"], k)
                    TT(xl[:, k - 1], xn[:, (k - 1) % 2], xh[:, k - 1].bitcast(F32), ALU.subtract)\
                        .then_inc(S["xl_out"], 1)
                if k in (3, 4):
                    split_low(v, k - 3)
            v.wait_ge(*done("scr_turned"))
            for i in range(3):
                ins = v.tensor_copy(xp4[:, :, :, i],
                                    bank(6, 12 * 24).rearrange("p (t b i) -> p t b i", t=12, i=3)[:, :, :, i])
                if i == 2:
                    ins.then_inc(*did("scr_out"))
                else:
                    link(ins)
            v.wait_ge(c_landed, 16 * 9)
            v.tensor_copy(cm[:], cmf[:]).then_inc(*did("masks_out"))
            v.wait_ge(*done("scr_out"))
            v.memset(pre[:, :, 0:3], 0.0).then_inc(*did("pre_zero"))

            def reduce_keys(n0, n):
                for i in range(n0, n0 + n):
                    b, r = divmod(i, 8)
                    v.wait_ge(S["k_prod"], i + 1)
                    v.tensor_reduce(lg[:, b, :, 2 * r:2 * r + 2].rearrange("p h g -> p g h"),
                                    ring[:, i % 4].rearrange("p g (h d) -> p g h d", d=DB), AX.X, ALU.add)\
                        .then_inc(S["k_red"], 1)

            rope = cf[:, K_ROPE:].rearrange("p (t c) -> p t c", t=5)

            def rotate(x, cos, sin, tmp, shape):
                x1, x2 = x[..., 0:HALF], x[..., HALF:ROT]
                ts = [tmp[i] for i in range(4)]
                link(TT(ts[0], x1, cos, ALU.mult))
                link(TT(ts[1], x2, sin, ALU.mult))
                link(TT(ts[2], x2, cos, ALU.mult))
                link(TT(ts[3], x1, sin, ALU.mult))
                link(TT(x1, ts[0], ts[1], ALU.subtract))
                return TT(x2, ts[2], ts[3], ALU.add)

            def sample_rotate(first):
                x = mts[:, first:first + WB].rearrange("b (h d) -> b h d", d=DB)
                cs = [bc(rope[0:NS, 4:5, o:o + HALF], [NS, HB, HALF]) for o in (0, HALF)]
                tmp = [s[0:NS, :].rearrange("b (h d) -> b h d", d=HALF) for s in (s1, s2, s3, s4)]
                return rotate(x, cs[0], cs[1], tmp, None)

            def conv(j):
                u = 13 + j
                v.wait_ge(unit_out, u + 1)
                if j >= 2:
                    v.wait_ge(S["tm_turned"], j - 1)
                c, x = cvr[:, j % 2], pre[:, j % 2]
                w = [fw[:, R_CW + 12 * i + j:R_CW + 12 * i + j + 1] for i in range(CW)]
                link(TS(c, x[:, 0:SEQ], w[0], None, ALU.mult))
                link(STT(c, x[:, 1:1 + SEQ], w[1], c, ALU.mult, ALU.add))
                link(STT(c, x[:, 2:2 + SEQ], w[2], c, ALU.mult, ALU.add))
                STT(c, x[:, 3:3 + SEQ], w[3], c, ALU.mult, ALU.add).then_inc(S["conv_out"], 1)

            n_red = 0
            moba_before = {}
            for u, (kind, j, _) in enumerate(UNITS1):
                if u + 2 <= U_GATE:
                    split_low(v, u + 2)
                if kind == "c":
                    conv(j)
                if u > 0 and UNITS1[u - 1][0] in "qkv":
                    m = (u - 1) - (1 if u - 1 > 4 else 0)
                    v.wait_ge(S["mq_turned"], m + 1)
                    v.tensor_copy(mts[:, m * P:(m + 1) * P], bank(6, P, NS)).then_inc(S["mts_out"], 1)
                if u == 4:
                    v.wait_ge(S["mts_out"], 4)
                    sample_rotate(0).then_inc(*did("rope_q"))
                if u == 5:
                    v.wait_ge(*done("ba_turned"))
                    link(v.tensor_copy(ba[:, 0:4, :], bank(7, 32).rearrange("p (t c) -> p t c", t=4)))
                    v.tensor_copy(ba[0:NS, 4, :], bank(7, 40, NS)[:, 32:40]).then_inc(*did("ba_out"))
                if u == 10:
                    v.wait_ge(S["mts_out"], 8)
                    v.wait_ge(*done("rope_q"))
                    sample_rotate(WB).then_inc(S["rope_k"], 1)
                    v.wait_ge(S["mt_out"], 8)
                    x = mtqk[:].rearrange("p t (h d) -> p t h d", d=DB)
                    tmp = [cvr[:, 0].rearrange("p (t c) -> p t c", t=4), cvr[:, 1].rearrange("p (t c) -> p t c", t=4)]
                    for half in range(2):
                        tmps = [t.rearrange("p t (h d) -> p t h d", d=HALF) for t in tmp]
                        xx = x[:, :, 8 * half:8 * half + 8, :]
                        c4 = [bc(rope[:, 0:4, o:o + HALF].rearrange("p t (o d) -> p t o d", o=1), [P, 4, HB, HALF])
                              for o in (0, HALF)]
                        quarter = [tmps[0][:, :, 0:8], tmps[0][:, :, 8:16], tmps[1][:, :, 0:8], tmps[1][:, :, 8:16]]
                        ins = rotate(xx, c4[0], c4[1], quarter, None)
                        if half:
                            ins.then_inc(S["rope_k"], 1)
                        else:
                            link(ins)
                    v.wait_ge(S["rope_k"], 2)
                    link(TT(s1[0:NS, :], s1[0:NS, :], s1[0:NS, :], ALU.mult))
                    t = cvr[0:NS, 0]
                    link(TT(t, mts[:, 0:WB], mts[:, WB:2 * WB], ALU.mult))
                    v.tensor_reduce(own[:], t.rearrange("b (h d) -> b h d", d=DB), AX.X, ALU.add)\
                        .then_inc(*did("own_out"))
                    v.wait_ge(*done("own_out"))
                if u >= RED_STEP0:
                    reduce_keys(n_red, 2)
                    n_red += 2

            link(TT(gg[:], ba[:, :, HA:], bc(dtb[:].rearrange("p (o h) -> p o h", o=1), [P, 5, HA]), ALU.add))
            link(TS(gt[:], gg[:], -1.0, None, ALU.mult))
            TT(gt[:], gg[:], gt[:], ALU.max).then_inc(*did("sp_in"))
            v.wait_ge(*done("sp_out"))
            link(TS(gg[:], gg[:], 0.0, None, ALU.max))
            link(TT(gg[:], gg[:], gt[:], ALU.add))
            link(TT(gg[:], gg[:], bc(alog[:].rearrange("p (o h) -> p o h", o=1), [P, 5, HA]), ALU.mult))
            link(TS(gg[:], gg[:], -1.0, None, ALU.mult))
            v.wait_ge(*done("sig_out"))
            TS(nbeta[:], beta[:], -1.0, None, ALU.mult).then_inc(*did("gate_ready"))

            def attention_out(c):
                v.wait_ge(S["att_pv"], HB * (c + 1))
                v.wait_ge(S["att_exp"], HB * (c + 1))
                link(v.reciprocal(rrs[:], rs[:, HB * c:HB * (c + 1)]))
                if c >= 1:
                    v.wait_ge(S["ob_turned"], c)
                TT(ob[:].rearrange("p (h d) -> p h d", d=DB), bank(6 + c % 2).rearrange("p (h d) -> p h d", d=DB),
                   bc(rrs[:].rearrange("p (h o) -> p h o", o=1), [P, HB, DB]), ALU.mult).then_inc(S["ob_out"], 1)

            def attention_low(c):
                v.wait_ge(S["onb_h_out"], c + 1)
                TT(onb_l[:, :, c * P:(c + 1) * P], bank(6 + c % 2).rearrange("p (t c) -> p t c", t=4),
                   onb_h[:, :, c * P:(c + 1) * P].bitcast(F32), ALU.subtract).then_inc(S["onb_l_out"], 1)

            for n in range(4 * HB):
                q_t, h = divmod(n, HB)
                N = (q_t + 1) * P
                v.wait_ge(S["att_sums"], n + 1)
                link(TT(bank(n % 4)[:, N - P:N], bank(n % 4)[:, N - P:N], cf[:, K_CAUS:K_CAUS + P], ALU.add))
                link(v.tensor_reduce(smx[:, n % 2:n % 2 + 1], bank(n % 4, N), AX.X, ALU.max))
                if n >= 2:
                    v.wait_ge(S["att_exp"], n - 1)
                TS(nbias[:, n % 2:n % 2 + 1], smx[:, n % 2:n % 2 + 1], -ATT_SCALE, None, ALU.mult)\
                    .then_inc(S["att_max"], 1)
                if n_red < GROUPS:
                    reduce_keys(n_red, 1)
                    n_red += 1
                if h == 1 and q_t >= 1:
                    attention_out(q_t - 1)
                if h == 4 and q_t >= 1:
                    attention_low(q_t - 1)
            attention_out(3)
            attention_low(3)

            split_low(v, U_GATE + 1)
            for half in range(2):
                v.wait_ge(S["sel_turned"], half + 1)
                src = bank(4 + half).rearrange("p (b l) -> p b l", b=4)
                link(v.tensor_reduce(s1[:, 4 * half:4 * half + 4], src, AX.X, ALU.max))
                ins = v.tensor_reduce(s1[:, 8 + 4 * half:12 + 4 * half], src, AX.X, ALU.add)
                if half:
                    ins.then_inc(*did("sel_red"))
                else:
                    link(ins)
            split_low(v, U_GATE + 2)
            v.wait_ge(*done("sel2_turned"))
            v.wait_ge(S["k_prod"], GROUPS)
            link(v.tensor_copy(pmt[:].rearrange("b a n -> b (a n)"), bank(6, 256, NS)))
            pair = pmt[:].rearrange("b a (n two) -> b a n two", two=2)
            link(TT(blk[:, 0, :], pair[:, 0, :, 0], pair[:, 0, :, 1], ALU.max))
            link(TT(blk[:, 1, :], pair[:, 1, :, 0], pair[:, 1, :, 1], ALU.add))
            sc = blk[:, 1, :].rearrange("b (h n) -> b h n", h=HB)
            s_m = bc(sc.rearrange("b h (o m) -> b h o m", o=1), [NS, HB, NBLK, NBLK])
            s_n = bc(sc.rearrange("b h (n o) -> b h n o", o=1), [NS, HB, NBLK, NBLK])
            g4 = gcmp[:].rearrange("b (h n m) -> b h n m", h=HB, n=NBLK)
            e4 = ecmp[:].rearrange("b (h n m) -> b h n m", h=HB, n=NBLK)
            link(TT(g4, s_m, s_n, ALU.is_gt))
            link(TT(e4, s_m, s_n, ALU.is_equal))
            split_low(v, U_GATE + 3)
            before = bc(cf[0:NS, K_LT8:K_LT8 + 64].rearrange("b (o n) -> b o n", o=1), [NS, HB, 64])
            link(TT(ecmp[:].rearrange("b (h n) -> b h n", h=HB), ecmp[:].rearrange("b (h n) -> b h n", h=HB),
                    before, ALU.mult))
            link(TT(gcmp[:], gcmp[:], ecmp[:], ALU.add))
            link(v.tensor_reduce(sel[:], gcmp[:].rearrange("b (n m) -> b n m", m=NBLK), AX.X, ALU.add))
            link(TS(sel[:], sel[:], TOPK - 0.5, None, ALU.is_lt))
            link(TS(sel[:], sel[:], BIG, -BIG, ALU.mult, ALU.add))
            link(TT(blk[:, 0, :], blk[:, 0, :], sel[:], ALU.add))
            link(v.tensor_reduce(s2[0:NS, 0:HB], blk[:, 0, :].rearrange("b (h n) -> b h n", h=HB), AX.X, ALU.max))
            link(TT(s2[0:NS, 0:HB], s2[0:NS, 0:HB], own[:], ALU.max))
            link(TT(sel[:].rearrange("b (h n) -> b h n", h=HB), sel[:].rearrange("b (h n) -> b h n", h=HB),
                    bc(s2[0:NS, 0:HB].rearrange("b (h o) -> b h o", o=1), [NS, HB, NBLK]), ALU.subtract))
            split_low(v, U_GATE + 4)
            link(v.tensor_copy(pair[:, 0], bc(sel[:].rearrange("b (n o) -> b n o", o=1), [NS, 64, 2])))
            link(TT(own[:], own[:], s2[0:NS, 0:HB], ALU.subtract))
            eye = cf[0:NS, K_ID:K_ID + NS]
            TT(bd8[:], bc(pmt[:, 0:1, :], [NS, NS, P]), bc(eye.rearrange("r (b o) -> r b o", o=1), [NS, NS, P]),
               ALU.mult).then_inc(*did("bias_ready"))
            v.wait_ge(*done("bias_sums"))
            TT(lg[:].rearrange("p b h g -> p (b h g)"), lg[:].rearrange("p b h g -> p (b h g)"), ps[:, 4 * 512:6 * 512],
               ALU.add).then_inc(*did("lg_biased"))
            split_low(v, U_GATE + 5)
            v.wait_ge(*done("lg_exp"))
            link(v.tensor_reduce(s1[:], lg[:].rearrange("p b h g -> p (b h) g"), AX.X, ALU.add))
            v.wait_ge(*done("own_exp"))
            TT(s2[0:NS, :].rearrange("r (b h) -> r b h", b=NS), bc(own[:].rearrange("r (o h) -> r o h", o=1), [NS, NS, HB]),
               bc(eye.rearrange("r (b o) -> r b o", o=1), [NS, NS, HB]), ALU.mult).then_inc(*did("row_sums"))
            split_low(v, U_GATE + 6)
            v.wait_ge(*done("den_sums"))
            link(v.tensor_copy(s3[:], bank(6, 128)[:, 64:128]))
            v.reciprocal(s4[:], bank(6, 64)).then_inc(*did("den_out"))
            v.wait_ge(*done("den_out"))

            v.wait_ge(*done("gc_sums"))
            v.tensor_copy(gc[:].rearrange("p c h -> p (c h)"), bank(7, NCH * HA)).then_inc(*did("gc_out"))
            split_low(v, U_GATE + 7)
            for c in range(NCH):
                v.wait_ge(S["sq_out"], c + 1)
                v.tensor_reduce(qks[:, c], sq4[:, c], AX.X, ALU.add).then_inc(S["sq_red"], 1)
            split_low(v, U_GATE + 8)
            v.wait_ge(S["sq_red"], NCH)
            TS(qks[:], qks[:], EPS, None, ALU.add).then_inc(*did("ssr_in"))
            v.wait_ge(*done("ssr_out"))
            link(v.reciprocal(qks[:], qks[:]))
            link(TS(qks[:, :, 0:HA], qks[:, :, 0:HA], Q_SCALE, None, ALU.mult))
            v.wait_ge(*done("egc_out"))
            link(TT(ckb[:], nbeta[:, 0:NCH], egc[:], ALU.mult))

            def wide(ap):
                return bc(ap.rearrange("p (h o) -> p h o", o=1), [P, HA, DA])

            def rows(ap):
                return bc(ap.rearrange("p (o c) -> p o c", o=1), [P, HA, P])

            def head4(ap):
                return ap.rearrange("p (h d) -> p h d", h=HA)

            for pr in range(NCH // 2):
                for p in range(2):
                    c = 2 * pr + p
                    if c == 0:
                        v.wait_ge(unit_done, U_GATE + 8)
                    TT(sq_[:, p], wide(gg[:, c]), rows(cf[:, K_TRI:K_TRI + P]), ALU.mult).then_inc(S["gu_ready"], 1)
                    v.wait_ge(S["gb_sums"], c + 1)
                    gb4 = head4(bank(4 + 2 * p))
                    link(TT(An[:, p], wide(gc[:, c]), gb4, ALU.subtract))
                    TT(An[:, p], An[:, p], rows(cf[:, K_STRICT:K_STRICT + P]), ALU.add).then_inc(S["dec_in"], 1)
                    link(TT(qkt[:, p], gb4, wide(gc[:, c]), ALU.subtract))
                    TT(qkt[:, p], qkt[:, p], rows(cf[:, K_INCT:K_INCT + P]), ALU.add).then_inc(S["dec_in"], 1)
                    last = gb4[:, :, P - 1]
                    link(v.tensor_copy(glx[:, c, 0:HA], last))
                    TT(glx[:, c, HA:], last, gc[:, c], ALU.subtract).then_inc(S["gl_in"], 1)
                for p in range(2):
                    c = 2 * pr + p
                    q, k, vv = (head4(tm[:, c, i * 512:(i + 1) * 512]) for i in range(3))
                    TT(q, q, wide(qks[:, c, 0:HA]), ALU.mult).then_inc(S["q_scaled"], 1)
                    TT(k, k, wide(qks[:, c, HA:]), ALU.mult).then_inc(S["k_scaled"], 1)
                    v.wait_ge(S["q_scaled"], c + 1)
                    TT(sq_[:, p], q, wide(egc[:, c]), ALU.mult).then_inc(S["qg_scaled"], 1)
                    link(TT(vv, vv, wide(beta[:, c]), ALU.mult))
                    v.wait_ge(S["q_turned"], c + 1)
                    v.wait_ge(S["qg_scaled"], c + 1)
                    v.wait_ge(S["k_scaled"], c + 1)
                    v.wait_ge(S["gl_out"], c + 1)
                    link(TT(q, k, wide(glx[:, c, HA:]), ALU.mult))
                    v.wait_ge(S["ktr_turned"], c + 1)
                    TT(k, k, wide(ckb[:, c]), ALU.mult).then_inc(S["k_ready"], 1)
                for p in range(2):
                    c = 2 * pr + p
                    v.wait_ge(S["kk_sums"], c + 1)
                    v.wait_ge(S["dec_n"], c + 1)
                    for h in range(HA):
                        ins = STT(An[:, p, h], head4(bank(4 + 2 * p))[:, h], nbeta[:, c, h:h + 1], An[:, p, h],
                                  ALU.mult, ALU.mult)
                    ins.then_inc(S["an_ready"], 1)
                    v.wait_ge(S["qk_sums"], c + 1)
                    v.wait_ge(S["dec_t"], c + 1)
                    TT(qkt[:, p], head4(bank(5 + 2 * p)), qkt[:, p], ALU.mult).then_inc(S["qkt_ready"], 1)
                    link(v.tensor_copy(Dm[:, p], rows(ident)))
                    v.wait_ge(S["an_ready"], c + 1)
                    v.copy_predicated(Dm[:, p], rows(cm[:, 0, 0]), An[:, p]).then_inc(S["d_ready"], 1)
                for lv in range(1, LEVELS):
                    for p in range(2):
                        n = 2 * ((LEVELS - 1) * pr + lv - 1) + p + 1
                        if lv == 1:
                            v.wait_ge(S["e_out"], 2 * pr + p + 1)
                            v.wait_ge(S["e_turned"], 2 * pr + p + 1)
                        v.wait_ge(S["lv_e"], n)
                        v.copy_predicated(Em[:, p], rows(cm[:, 1, lv]), head4(bank(4 + 2 * p))).then_inc(S["lv_e_out"], 1)
                        if lv < LEVELS - 1:
                            v.wait_ge(S["lv_d"], 2 * ((LEVELS - 2) * pr + lv - 1) + p + 1)
                            v.copy_predicated(Dm[:, p], rows(cm[:, 0, lv]), head4(bank(5 + 2 * p)))\
                                .then_inc(S["lv_d_out"], 1)
                for p in range(2):
                    c = 2 * pr + p
                    v.wait_ge(S["s_sums"], c + 1)
                    if c == 0:
                        v.tensor_copy(st[:, 1], head4(bank(p))).then_inc(S["s_out"], 1)
                    else:
                        v.wait_ge(S["s_out"], c)
                        for h in range(HA):
                            ins = STT(st[:, (c + 1) % 2, h], st[:, c % 2, h], glx[:, c, h:h + 1],
                                      head4(bank(p))[:, h], ALU.mult, ALU.add)
                        ins.then_inc(S["s_out"], 1)
                    v.wait_ge(S["osq_out"], c + 1)
                    link(v.tensor_reduce(on_st[:], sq_[:, p], AX.X, ALU.add))
                    TS(on_st[:], on_st[:], 1.0 / DA, EPS, ALU.mult, ALU.add).then_inc(S["on_ms"], 1)
                    v.wait_ge(S["on_root"], c + 1)
                    link(v.reciprocal(on_st[:], on_st[:]))
                    TT(sq_[:, p], head4(bank(5 + 2 * p)), wide(on_st[:]), ALU.mult).then_inc(S["on_ready"], 1)
                    v.wait_ge(S["on_turned"], c + 1)
                    for h in range(HA):
                        ins = STT(An[:, p, h], head4(bank(4 + 2 * p))[:, h], fw[:, R_DN:R_DN + 1],
                                  zs[:, h, c * P:(c + 1) * P], ALU.mult, ALU.mult)
                    ins.then_inc(S["on_gated"], 1)
                    v.wait_ge(S["ona_h_out"], c + 1)
                    TT(ona_l[:, :, c * P:(c + 1) * P], An[:, p], ona_h[:, :, c * P:(c + 1) * P].bitcast(F32),
                       ALU.subtract).then_inc(S["ona_l_out"], 1)

            link(v.tensor_copy(xp4[:, :, :, 3], tail[:, :, 3:]))
            wcv = fw[:, R_CW:R_CW + 48].rearrange("p (i t) -> p t i", t=12)
            for i in range(CW):
                link(TT(xp4[:, :, :, i], xp4[:, :, :, i],
                        bc(wcv[:, :, i:i + 1], [P, 12, NS]), ALU.mult))
            v.tensor_reduce(cvs[:], xp4[:], AX.X, ALU.add).then_inc(*did("sm_conv"))
            split_low(v, U_GATE + 9)
            v.wait_ge(*done("sm_sums"))
            TS(s1[:], bank(4, 64), EPS, None, ALU.add).then_inc(*did("sm_ms"))
            split_low(v, U_GATE + 10)
            v.wait_ge(*done("sm_root"))
            link(v.reciprocal(s1[:], s1[:]))
            link(TT(cvs[:, 0:8].rearrange("p t b -> p (t b)"), cvs[:, 0:8].rearrange("p t b -> p (t b)"), s1[:], ALU.mult))
            link(TS(cvs[:, 0:4], cvs[:, 0:4], Q_SCALE, None, ALU.mult))
            link(v.tensor_copy(s6[:].rearrange("p (b h) -> p b h", h=HA), cvs[:, 4:8].rearrange("p h b -> p b h")))
            v.wait_ge(*done("sm_bdin"))
            eye3 = bc(eye.rearrange("r (b o) -> r b o", o=1), [NS, NS, HA])
            link(TT(s1[0:NS, 0:32].rearrange("r (b h) -> r b h", b=NS),
                    bc(s5[0:NS, 0:HA].rearrange("r (o h) -> r o h", o=1), [NS, NS, HA]), eye3, ALU.mult))
            TT(s1[0:NS, 32:64].rearrange("r (b h) -> r b h", b=NS),
               bc(beta[0:NS, 4:5, :], [NS, NS, HA]), eye3, ALU.mult).then_inc(*did("sm_bd"))
            split_low(v, U_GATE + 11)
            v.wait_ge(*done("sm_bsums"))
            link(v.tensor_copy(s2[:], bank(6, 64)))
            v.wait_ge(st_landed, 16)
            TT(state[:], state[:], bc(s2[:, 0:32].rearrange("p (n o) -> p n o", o=1), [P, 32, DA]), ALU.mult)\
                .then_inc(*did("sm_decay"))
            split_low(v, U_GATE + 12)
            v.wait_ge(*done("sm_kv"))
            link(TT(s5[:].rearrange("p (b h) -> p b h", h=HA), cvs[:, 8:12].rearrange("p h b -> p b h"),
                    bank(7, 32).rearrange("p (b h) -> p b h", h=HA), ALU.subtract))
            TT(s5[:], s5[:], s2[:, 32:64], ALU.mult).then_inc(*did("sm_dlt"))
            split_low(v, U_GATE + 13)
            v.wait_ge(*done("sm_t1o"))
            TT(bd[:], bc(dlt[:].rearrange("r (o e) -> r o e", o=1), [32, 32, DA]),
               bc(cf[0:32, K_ID:K_ID + 32].rearrange("r (n o) -> r n o", o=1), [32, 32, DA]), ALU.mult)\
                .then_inc(*did("sm_bdo"))
            split_low(v, U_GATE + 14)
            for n in range(8):
                v.wait_ge(S["sm_outer"], n + 1)
                if n == 0:
                    v.wait_ge(*done("sm_decay"))
                TT(state[:, 4 * n:4 * n + 4], state[:, 4 * n:4 * n + 4], head4(bank(6 + n % 2)), ALU.add)\
                    .then_inc(S["sm_outer_out"], 1)
            split_low(v, U_GATE + 15)
            v.wait_ge(*done("sm_osum"))
            TS(s2[:, 0:32], bank(5, 32), 1.0 / DA, EPS, ALU.mult, ALU.add).then_inc(*did("sm_oms"))
            v.wait_ge(*done("sm_oroot"))
            link(v.reciprocal(s2[:, 0:32], s2[:, 0:32]))
            link(TT(s2[:, 0:32], s2[:, 0:32], bank(4, 32), ALU.mult))
            o_hb = s2[:, 0:32].rearrange("p (b h) -> p h b", h=HA)
            STT(s1[:, 0:32].rearrange("p (h b) -> p h b", h=HA), o_hb, fw[:, R_DN:R_DN + 1], zs[:, :, SEQ:NT],
                ALU.mult, ALU.mult).then_inc(v_own, 1)
            link.n += 1
            v.wait_ge(v_own, link.n)
            v.wait_ge(S["pv_done"], GROUPS)
            v.wait_ge(S["vn_out"], 4)
            for hh in range(2):
                sl = slice(64 * hh, 64 * hh + 64)
                w_own = s3[sl, :].rearrange("p (b c e) -> p c b e", b=NS, e=2)[:, :, :, hh]
                w_den = s4[sl, :].rearrange("p (b c e) -> p c b e", b=NS, e=2)[:, :, :, hh]
                o4 = s5[sl, :].rearrange("p (c b) -> p c b", c=4)
                link(TT(o4, w_own, vnew_s[sl], ALU.mult))
                link(TT(o4, o4, ps[sl, 2 * 512:2 * 512 + 64].rearrange("p (c b e) -> p c b e", c=4, e=2)[:, :, :, hh],
                        ALU.add))
                link(TT(s6[sl, :].rearrange("p (c b) -> p c b", c=4), o4, w_den, ALU.mult))
            split_low(v, U_GATE + 16)
            link(v.tensor_copy(s3[:, 0:32], s1[:, 0:32]))
            v.tensor_copy(s4[:, 0:32], s6[:]).then_inc(*did("sm_on"))
            v.wait_ge(*done("sm_on"))
            v.wait_ge(*done("sm_oh"))
            TT(ona_l[:, :, SEQ:NT], s3[:, 0:32].rearrange("p (h b) -> p h b", h=HA), ona_h[:, :, SEQ:NT].bitcast(F32),
               ALU.subtract).then_inc(*did("os_ready"))
            v.wait_ge(*done("os_h"))
            TT(onb_l[:, :, SEQ:NT], s4[:, 0:32].rearrange("p (c b) -> p c b", c=4), onb_h[:, :, SEQ:NT].bitcast(F32),
               ALU.subtract).then_inc(*did("os_l"))

            split_low(v, U_MERGE + 1)
            for j in range(8):
                u = U_MERGE + j
                v.wait_ge(unit_done, u + 1)
                v.wait_ge(S["gate_out"], 16)
                b = 2 * (1 - j % 2)
                link(TT(sga[:], unit_ps(b), gate_a[:, j], ALU.mult))
                link(TT(sgb[:], unit_ps(b + 1), gate_b[:, j], ALU.mult))
                if j >= 1:
                    v.wait_ge(S["mh_out"], j)
                TT(mx_[:], sga[:], sgb[:], ALU.add).then_inc(S["mix_ready"], 1)
                split_low(v, u + 2)
                v.wait_ge(S["mix_ready"], j + 1)
                v.wait_ge(S["mh_out"], j + 1)
                TT(ml[:, j], mx_[:], mh[:, j].bitcast(F32), ALU.subtract).then_inc(S["ml_out"], 1)
                v.wait_ge(S["ml_out"], j + 1)

            for j in range(8):
                v.wait_ge(unit_done, U_OUT + j + 1)
                v.wait_ge(ht_landed, 16 * (j + 1))
                TT(ht[:, j], unit_ps((U_OUT + j) % 2), ht[:, j], ALU.add).then_inc(S["h_out"], 1)
                split_low(v, U_OUT + j + 2)
                v.wait_ge(S["sq2_out"], j + 1)
                if j == 0:
                    v.wait_ge(stored, 48)
                    v.tensor_copy(ssum[:], sqh[:, 0]).then_inc(S["ssum_ready"], 1)
                else:
                    v.wait_ge(S["ssum_ready"], j)
                    TT(ssum[:], ssum[:], sqh[:, j % 2], ALU.add).then_inc(S["ssum_ready"], 1)
                v.wait_ge(S["hx_h"], j + 1)
                STT(xl[:, j], ht[:, j], fw[:, R_N2 + j:R_N2 + j + 1], xh[:, j].bitcast(F32), ALU.mult, ALU.subtract)\
                    .then_inc(S["hx_l"], 1)
            v.wait_ge(*done("ss_sums"))
            link(TS(rb[:], unit_ps(2), 1.0 / DM, EPS, ALU.mult, ALU.add))
            v.reciprocal(rb[:], rb[:]).then_inc(*did("inv_ready"))
            v.wait_ge(*done("inv_ready"))

            def mlp(g, last=False):
                for i in range(16):
                    if 1 <= i <= 8:
                        v.wait_ge(S["uh_out"], g * 8 + i)
                        TT(ml[:, i - 1], uu[:, (i - 1) % 2], mh[:, i - 1].bitcast(F32), ALU.subtract)\
                            .then_inc(S["ul_out"], 1)
                    if i >= 8:
                        j = i - 8
                        v.wait_ge(unit_done, g * 16 + (U_MLP + i + 1))
                        TT(ht[:, j], unit_ps((U_MLP + i) % 2), ht[:, j], ALU.add).then_inc(S["h_out"], 1)
                    if not (last and i >= 14):
                        split_low(v, U_MLP + i + 2, g * 16)
                    if i < 8:
                        v.wait_ge(S["relsq_out"], g * 8 + (i + 1))
                        TT(uu[:, i % 2], rel[:, i % 2], rb[:], ALU.mult).then_inc(S["uu_ready"], 1)
                        v.wait_ge(S["uu_ready"], g * 8 + (i + 1))
            with v.Fori(0, 3) as g:
                mlp(g)
            mlp(3, True)

            v.wait_ge(wf_landed, 16)
            for t in range(5):
                n = P if t < 4 else NS
                v.wait_ge(S["y_sq"], t + 1)
                TS(ss[0:n, t:t + 1], ss[0:n, t:t + 1], 1.0 / DM, EPS, ALU.mult, ALU.add).then_inc(S["y_ms"], 1)
                v.wait_ge(S["y_root"], t + 1)
                link(v.reciprocal(rstd[0:n, t:t + 1], rstd[0:n, t:t + 1]))
                if t >= 2:
                    v.wait_ge(stored, 16 * (2 + t))
                STT(yy[0:n, t % 2], ps[0:n, (t % 4) * 1024:(t % 4) * 1024 + DM], rstd[0:n, t:t + 1], wf[0:n, :],
                    ALU.mult, ALU.mult).then_inc(S["y_out"], 1)

        @block.tensor
        def _(pe):
            mm, tr = pe.matmul, pe.transpose

            def turn4(dst_bank, srcs, n=P):
                for i, s in enumerate(srcs):
                    last = tr(bank(dst_bank)[:, i * P:(i + 1) * P], s, ident)
                return last

            pe.wait_ge(c_landed, 16 * 9)
            tr(ps[:, 1024:1024 + R_N], wr[:], cf[0:R_N, K_ID:K_ID + R_N]).then_inc(*did("fw_turned"))
            for t in range(5):
                pe.wait_ge(x_landed[t], 16)
            for k in range(KT):
                if k >= 3:
                    pe.wait_ge(S["ht_out"], k - 2)
                if k == 1:
                    pe.wait_ge(*done("fw_out"))
                for t in range(5):
                    n = P if t < 4 else NS
                    last = tr(unit_ps(k % 3)[:, t * P:t * P + n], xin[0:n, t, k * P:(k + 1) * P], cf[0:n, K_ID:K_ID + n])
                last.then_inc(S["xt_turned"], 1)
                if k == 0:
                    pe.wait_ge(*done("rstd_ready"))
                    for t in range(5):
                        n = P if t < 4 else NS
                        last = mm(unit_ps(3)[:, t * P:t * P + n], bc(rstd[0:n, t:t + 1], [n, P]),
                                  cf[0:n, K_ID:K_ID + n], start=True, stop=True, skip_group_check=True)
                    last.then_inc(*did("rb_sums"))

            pe.wait_ge(*done("rb_out"))
            for t in range(12):
                last = tr(bank(6)[:, t * 24:(t + 1) * 24], scr[:, t * P:(t + 1) * P], cf[0:24, K_ID:K_ID + 24])
            last.then_inc(*did("scr_turned"))

            def turn_moba(m):
                u = m if m < 4 else m + 1
                pe.wait_ge(unit_out, u + 1)
                if m >= 2:
                    pe.wait_ge(S["mt_out"], m - 1)
                if m >= 1:
                    pe.wait_ge(S["mts_out"], m)
                if m == 0:
                    pe.wait_ge(*done("scr_out"))
                if m == 4:
                    pe.wait_ge(S["qb_out"], NS)
                turn4(4 + m % 2, [mq[:, m % 2, t * P:(t + 1) * P] for t in range(4)])
                tr(bank(6, P, NS), mq[:, m % 2, SEQ:NT], ident).then_inc(S["mq_turned"], 1)

            def turn_conv(j):
                pe.wait_ge(S["silu_out"], j + 1)
                if j >= 2:
                    pe.wait_ge(S["tm_out"], j - 1)
                else:
                    pe.wait_ge(S["mt_out"], 12)
                turn4(4 + j % 2, [cvr[:, j % 2, t * P:(t + 1) * P] for t in range(4)]).then_inc(S["tm_turned"], 1)

            for u, (kind, j, _) in enumerate(UNITS1):
                pe.wait_ge(S_lo, u + 1)
                if u >= 2:
                    pe.wait_ge(unit_out, u - 1)
                if u == 0:
                    pe.wait_ge(S["ht_out"], KT)
                    product(pe, u, unit_ps(u % 2), xh, xl, before_k=lambda k: pe.wait_ge(S["xl_out"], k + 1))\
                        .then_inc(unit_done, 1)
                else:
                    product(pe, u, unit_ps(u % 2), xh, xl).then_inc(unit_done, 1)
                if u == 5:
                    pe.wait_ge(unit_out, 5)
                    for t in range(5):
                        n = P if t < 4 else NS
                        last = tr(bank(7)[0:n, 8 * t:8 * t + 8], baf[:, t * P:t * P + n], cf[0:8, K_ID:K_ID + 8])
                    last.then_inc(*did("ba_turned"))
                    pe.wait_ge(*done("rope_q"))
                if u in (5, 6):
                    for b in range(4 * (u - 5), 4 * (u - 5) + 4):
                        if b == 0:
                            pe.wait_ge(S["mt_out"], 4)
                            pe.wait_ge(S["mts_out"], 4)
                        if b == 3:
                            pe.wait_ge(*done("ba_out"))
                        if b >= 4:
                            pe.wait_ge(S["qb_out"], b - 3)
                        mm(bank(4 + b % 4), bc(cf[0:NS, K_ID + b:K_ID + b + 1], [NS, P]), mts[:, 0:WB],
                           start=True, stop=True).then_inc(S["qb_sums"], 1)
                if u >= 1 and UNITS1[u - 1][0] in "qkv":
                    turn_moba((u - 1) - (1 if u - 1 > 4 else 0))
                if kind == "c" and j >= 2:
                    turn_conv(j - 2)
                if kind == "z" and j < 2:
                    turn_conv(10 + j)

            pe.wait_ge(unit_out, N1)
            pe.wait_ge(S["rope_k"], 2)
            for n in range(8):
                if n >= 4:
                    pe.wait_ge(S["qk_out"], n - 3)
                turn4(n % 4, [mtqk[:, t, n * P:(n + 1) * P] for t in range(4)]).then_inc(S["qk_turned"], 1)

            def scores(n):
                q_t, h = divmod(n, HB)
                r, N = slice(64 * (h % 2), 64 * (h % 2) + 64), (q_t + 1) * P
                if n < 4:
                    pe.wait_ge(S["qk_out"], 8)
                else:
                    pe.wait_ge(S["att_exp"], n - 3)
                mm(bank(n % 4, N), qt[r, h // 2, q_t * P:(q_t + 1) * P], kt[r, h // 2, 0:N], start=True, stop=True)\
                    .then_inc(S["att_sums"], 1)

            def turn_probs(n):
                pe.wait_ge(S["att_exp"], n + 1)
                if n >= 2:
                    pe.wait_ge(S["pt_out"], n - 1)
                else:
                    pe.wait_ge(S["tm_out"], 12)
                for t in range(n // HB + 1):
                    last = tr(bank(4 + n % 2)[:, t * P:(t + 1) * P], prob[:, n % 2, t * P:(t + 1) * P], ident)
                last.then_inc(S["pt_turned"], 1)

            def pv_prompt(n):
                q_t, h = divmod(n, HB)
                pe.wait_ge(S["pt_out"], n + 1)
                if h == 0 and q_t >= 2:
                    pe.wait_ge(S["onb_l_out"], q_t - 1)
                if n == 0:
                    pe.wait_ge(S["mts_out"], 12)
                for t in range(q_t + 1):
                    last = mm(bank(6 + q_t % 2)[:, h * DB:(h + 1) * DB], probt[:, n % 2, t * P:(t + 1) * P],
                              mtv[:, t, h * DB:(h + 1) * DB], start=(t == 0), stop=(t == q_t), skip_group_check=True)
                last.then_inc(S["att_pv"], 1)

            def turn_ob(c):
                pe.wait_ge(S["ob_out"], c + 1)
                turn4(6 + c % 2, [ob[:, t * P:(t + 1) * P] for t in range(4)]).then_inc(S["ob_turned"], 1)

            NA = 4 * HB
            for n in range(3):
                scores(n)
            for n in range(NA + 1):
                if n + 3 < NA:
                    scores(n + 3)
                if n < NA:
                    turn_probs(n)
                if n >= 1:
                    pv_prompt(n - 1)
                if n % HB == 2 and n > HB:
                    turn_ob(n // HB - 1)
            turn_ob(3)

            pe.wait_ge(S["att_exp"], NA)
            pe.wait_ge(S["onb_h_out"], 4)
            pe.wait_ge(S["pt_out"], NA)
            pe.wait_ge(S["onb_l_out"], 4)
            for t in range(12):
                last = tr(ps[0:3 + NS, 5 * 512 + t * P:5 * 512 + (t + 1) * P], tail[:, t, :], ident)
            last.then_inc(*did("tail_turned"))

            def gate(n):
                u = U_GATE + n
                pe.wait_ge(S_lo, u + 1)
                if n >= 2:
                    pe.wait_ge(S["gate_out"], n - 1)
                product(pe, u, unit_ps(u % 2), xh, xl).then_inc(unit_done, 1)

            gate(0)
            pe.wait_ge(S["k_red"], GROUPS)
            pe.wait_ge(*done("tail_out"))
            for b in range(NS):
                last = tr(bank(4 + b // 4)[:, (b % 4) * P:(b % 4 + 1) * P], lg[:, b].rearrange("p h g -> p (h g)"), ident)
                if b % 4 == 3:
                    last.then_inc(S["sel_turned"], 1)
            gate(1)
            pe.wait_ge(*done("sel_red"))
            tr(bank(6, P, NS), s1[:, 0:8], ident)
            tr(bank(6, 2 * P, NS)[:, P:2 * P], s1[:, 8:16], ident).then_inc(*did("sel2_turned"))
            gate(2)
            gate(3)
            pe.wait_ge(*done("bias_ready"))
            for i in range(2):
                last = mm(bank(4 + i), cf[0:NS, K_ONE:K_ONE + P], bd8[:, 4 * i:4 * i + 4, :].rearrange("r b n -> r (b n)"),
                          start=True, stop=True)
            last.then_inc(*did("bias_sums"))
            gate(4)
            pe.wait_ge(*done("row_sums"))
            mm(bank(6, 64), ones, s1[:], start=True, stop=False, skip_group_check=True)
            mm(bank(6, 64), cf[0:NS, K_ONE:K_ONE + P], s2[0:NS, :], start=False, stop=True, skip_group_check=True)
            mm(bank(6, 128)[:, 64:128], cf[0:NS, K_ONE:K_ONE + P], s2[0:NS, :], start=True, stop=True,
               skip_group_check=True).then_inc(*did("den_sums"))
            pe.wait_ge(*done("gate_ready"))
            mm(bank(7, NCH * HA), cf[:, K_TRI:K_TRI + P], gg[:, 0:NCH].rearrange("p c h -> p (c h)"), start=True,
               stop=True).then_inc(*did("gc_sums"))
            for n in (5, 6, 7):
                gate(n)

            pe.wait_ge(*done("lg_exp"))
            pe.wait_ge(S["gate_out"], 8)

            values_done = [0]

            def values(n):
                for g in range(values_done[0], min(values_done[0] + n, GROUPS)):
                    b, r = divmod(g, 8)
                    pe.wait_ge(kv_landed[r % 4], 16 * 2 * (2 * NS + 2 * b + r // 4 + 1))
                    for i in range(2):
                        for c in range(4):
                            col = 2 * 512 + c * 16 + b * 2
                            last = mm(ps[:, col:col + 2], ring[:, r % 4, i, c * P:(c + 1) * P],
                                      lg[:, b, 2 * c:2 * c + 2, 2 * r + i], start=(g == 0 and i == 0 and c == 0),
                                      stop=(g == GROUPS - 1 and i == 1 and c == 3), skip_group_check=True)
                    last.then_inc(S["pv_done"], 1)
                values_done[0] += n

            def heads(out, pairs):
                for h in range(HA):
                    for i, (left, right) in enumerate(pairs):
                        last = mm(bank(out)[:, h * P:(h + 1) * P], left(h), right(h), start=(i == 0),
                                  stop=(i == len(pairs) - 1), skip_group_check=True)
                return last

            for pr in range(NCH // 2):
                for p in range(2):
                    c = 2 * pr + p
                    pe.wait_ge(S["gu_ready"], c + 1)
                    if pr:
                        pe.wait_ge(S["ona_l_out"], 2 * pr)
                    elif p:
                        pe.wait_ge(*done("den_out"))
                        pe.wait_ge(*done("gc_out"))
                    mm(bank(4 + 2 * p), ones, sq_[:, p].rearrange("p h c -> p (h c)"), start=True, stop=True)\
                        .then_inc(S["gb_sums"], 1)
                values(4)
                for p in range(2):
                    c = 2 * pr + p

                    def part(i):
                        return [tm[:, c, i * 512 + h * P:i * 512 + (h + 1) * P] for h in range(HA)]
                    pe.wait_ge(S["q_scaled"], c + 1)
                    pe.wait_ge(S["gl_in"], c + 1)
                    turn4(4 + 2 * p, part(0)).then_inc(S["q_turned"], 1)
                    pe.wait_ge(S["k_scaled"], c + 1)
                    turn4(5 + 2 * p, part(1)).then_inc(S["ktr_turned"], 1)
                    pe.wait_ge(S["qg_scaled"], c + 1)
                    if pr:
                        pe.wait_ge(S["s_out"], 2 * pr)
                    turn4(p, [sq_[:, p, h] for h in range(HA)]).then_inc(S["qg_turned"], 1)
                for p in range(2):
                    c = 2 * pr + p
                    pe.wait_ge(S["kt_out"], c + 1)
                    heads(4 + 2 * p, [(lambda h: Em[:, p, h], lambda h: Em[:, p, h])]).then_inc(S["kk_sums"], 1)
                    heads(5 + 2 * p, [(lambda h: Em[:, p, h], lambda h: Dm[:, p, h])]).then_inc(S["qk_sums"], 1)
                values(4)
                for p in range(2):
                    c = 2 * pr + p
                    pe.wait_ge(S["d_ready"], c + 1)
                    turn4(4 + 2 * p, [Dm[:, p, h] for h in range(HA)]).then_inc(S["e_turned"], 1)
                for lv in range(1, LEVELS):
                    for p in range(2):
                        n = 2 * ((LEVELS - 1) * pr + lv - 1) + p
                        if lv == 1:
                            pe.wait_ge(S["e_out"], 2 * pr + p + 1)
                            pe.wait_ge(S["qgt_out"], 2 * pr + p + 1)
                        else:
                            pe.wait_ge(S["lv_e_out"], n - 1)
                        heads(p, [(lambda h: An[:, p, h], lambda h: Em[:, p, h])]).then_inc(S["lv_q"], 1)
                    values(2)
                    for p in range(2):
                        n = 2 * ((LEVELS - 1) * pr + lv - 1) + p
                        nd = 2 * ((LEVELS - 2) * pr + lv - 1) + p
                        pe.wait_ge(S["lv_q_out"], n + 1)
                        if lv > 1:
                            pe.wait_ge(S["lv_d_out"], nd - 1)
                        else:
                            pe.wait_ge(S["qkt_ready"], 2 * pr + p + 1)
                        heads(4 + 2 * p, [(lambda h: Dm[:, p, h], lambda h: sq_[:, p, h])]).then_inc(S["lv_e"], 1)
                        if lv < LEVELS - 1:
                            heads(5 + 2 * p, [(lambda h: sq_[:, p, h], lambda h: Dm[:, p, h])]).then_inc(S["lv_d"], 1)
                for p in range(2):
                    c = 2 * pr + p
                    pe.wait_ge(S["lv_e_out"], 2 * (LEVELS - 1) * pr + 2 * (LEVELS - 2) + p + 1)
                    pe.wait_ge(S["k_ready"], c + 1)
                    heads(p, [(lambda h: tm[:, c, 512 + h * P:512 + (h + 1) * P], lambda h: Em[:, p, h])])\
                        .then_inc(S["wt_sums"], 1)
                for p in range(2):
                    c = 2 * pr + p
                    pe.wait_ge(S["wt_out"], c + 1)
                    if c:
                        pe.wait_ge(S["s_out"], c)
                    with_state = [(lambda h: Dm[:, p, h], lambda h: st[:, c % 2, h])] if c else []
                    heads(4 + 2 * p, [(lambda h: Em[:, p, h], lambda h: tm[:, c, 1024 + h * P:1024 + (h + 1) * P])]
                          + with_state).then_inc(S["vn_sums"], 1)
                    values(3)
                    pe.wait_ge(S["vn_new"], c + 1)
                    heads(p, [(lambda h: tm[:, c, h * P:(h + 1) * P], lambda h: vnew[:, h])]).then_inc(S["s_sums"], 1)
                    from_state = [(lambda h: qgt[:, p, h], lambda h: st[:, c % 2, h])] if c else []
                    heads(5 + 2 * p, from_state + [(lambda h: qkt[:, p, h], lambda h: vnew[:, h])])\
                        .then_inc(S["o_sums"], 1)
                    values(3)
                    pe.wait_ge(S["on_ready"], c + 1)
                    turn4(4 + 2 * p, [sq_[:, p, h] for h in range(HA)]).then_inc(S["on_turned"], 1)

            values(GROUPS)
            pe.wait_ge(S["on_gated"], NCH)
            gate(8)
            pe.wait_ge(*done("sm_silu"))
            mm(bank(4, 64), ones, s1[:], start=True, stop=True).then_inc(*did("sm_sums"))
            gate(9)
            pe.wait_ge(*done("sm_bd"))
            mm(bank(6, 64), cf[0:NS, K_ONE:K_ONE + P], s1[0:NS, :], start=True, stop=True).then_inc(*did("sm_bsums"))
            gate(10)
            pe.wait_ge(*done("sm_decay"))
            for b in range(NS):
                for h in range(HA):
                    n = b * HA + h
                    last = mm(bank(7)[:, n:n + 1], state[:, n], s6[:, n:n + 1], start=True, stop=True,
                              skip_group_check=True)
            last.then_inc(*did("sm_kv"))
            gate(11)
            pe.wait_ge(*done("sm_dlt"))
            tr(bank(4, P, 32), s5[:], ident).then_inc(S["sm_t1"], 1)
            tr(bank(5, P, 32), s6[:], ident).then_inc(S["sm_t1"], 1)
            gate(12)
            pe.wait_ge(*done("sm_bdo"))
            for n in range(8):
                if n >= 2:
                    pe.wait_ge(S["sm_outer_out"], n - 1)
                mm(bank(6 + n % 2), knt[:], bd[:, 4 * n:4 * n + 4, :].rearrange("r n e -> r (n e)"), start=True, stop=True)\
                    .then_inc(S["sm_outer"], 1)
            gate(13)
            pe.wait_ge(S["sm_outer_out"], 8)
            for b in range(NS):
                for h in range(HA):
                    n = b * HA + h
                    last = mm(bank(4)[:, n:n + 1], state[:, n], cvs[:, h, b:b + 1], start=True, stop=True,
                              skip_group_check=True)
            last.then_inc(*did("sm_o"))
            gate(14)
            pe.wait_ge(*done("sm_osq"))
            mm(bank(5, 32), ones, s1[:, 0:32], start=True, stop=True).then_inc(*did("sm_osum"))
            gate(15)

            pe.wait_ge(*done("os_l"))
            for j in range(8):
                u, b = U_MERGE + j, 2 * (1 - j % 2)
                pe.wait_ge(S_lo, u + 1)
                if j == 1:
                    pe.wait_ge(S["gate_out"], 16)
                elif j >= 2:
                    pe.wait_ge(S["mix_ready"], j - 1)
                product(pe, u, unit_ps(b), ona_h, ona_l, range(4))
                product(pe, u, unit_ps(b + 1), onb_h, onb_l, range(4, 8)).then_inc(unit_done, 1)
            for j in range(8):
                u = U_OUT + j
                pe.wait_ge(S_lo, u + 1)
                if j >= 2:
                    pe.wait_ge(S["h_out"], j - 1)
                else:
                    pe.wait_ge(S["mix_ready"], 8)
                product(pe, u, unit_ps(u % 2), mh, ml,
                        before_k=(lambda k: pe.wait_ge(S["ml_out"], k + 1)) if j == 0 else None).then_inc(unit_done, 1)

            def mlp(g):
                for i in range(16):
                    u = U_MLP + i
                    pe.wait_ge(S_lo, g * 16 + (u + 1))
                    if i < 2 or i >= 10:
                        pe.wait_ge(S["h_out"], g * 8 + (7 + i if i < 2 else 8 + i - 9))
                    else:
                        pe.wait_ge(S["rel_out"], g * 8 + (i - 1))
                    wait_u = (lambda k: pe.wait_ge(S["ul_out"], g * 8 + (k + 1))) if i == 8 else None
                    if i == 0:
                        wait_u = lambda k: pe.wait_ge(S["hx_l"], k + 1)
                    rh, rl = (xh, xl) if i < 8 else (mh, ml)
                    product(pe, u, unit_ps(u % 2), rh, rl, before_k=wait_u).then_inc(unit_done, 1)
                    if i == 0 and isinstance(g, int):
                        pe.wait_ge(S["ssum_ready"], 8)
                        for a, b in ((0, 256), (256, NT)):
                            last = mm(unit_ps(2)[:, a:b], ones, ssum[:, a:b], start=True, stop=True)
                        last.then_inc(*did("ss_sums"))
            mlp(0)
            with pe.Fori(1, 4) as g:
                mlp(g)

            pe.wait_ge(S["h_out"], 8 + 32)
            for t in range(5):
                n = P if t < 4 else NS
                if t == 4:
                    pe.wait_ge(S["y_out"], 1)
                for k in range(KT):
                    col = (t % 4) * 1024 + k * P
                    last = tr(ps[0:n, col:col + P], ht[:, k, t * P:t * P + n], ident)
                last.then_inc(S["yt_turned"], 1)


_INS = ["x_prompt", "x_sample", "cache_k", "cache_v", "page_table", "state_delta", "state_conv", "norm1_w", "w_in",
        "conv_w", "a_log", "dt_bias", "delta_norm_w", "w_proj_a", "w_proj_b", "w_out", "norm2_w", "w_up", "w_down",
        "norm_f_w"]
_OUTS = [(1, SEQ, DM), (NS, 1, DM), (1, 1, SEQ, HB, DB), (1, 1, SEQ, HB, DB), (1, 1, HA, DA, DA),
         (1, 1, CW - 1, CC), (1, NS, 1, HB, DB), (1, NS, 1, HB, DB), (1, NS, HA, DA, DA), (1, NS, CW - 1, CC)]


def kernel(**inputs):
    import concourse.bacc as _bacc
    from concourse.bass_utils import run_bass_kernel_spmd as _run

    nc = _bacc.Bacc("TRN2", target_bir_lowering=False, num_devices=1)
    const_f, const_m = constants()
    arrays, args = {}, []
    named = [("const_f", const_f), ("const_m", const_m)] + [(n, inputs[n]) for n in _INS]
    for name, a in named:
        a = np.ascontiguousarray(a)
        arrays[f"in_{name}"] = a
        args.append(nc.dram_tensor(f"in_{name}", a.shape, mybir.dt.from_np(a.dtype), kind="ExternalInput").ap())
    for i, shape in enumerate(_OUTS):
        args.append(nc.dram_tensor(f"out_{i}", shape, F32, kind="ExternalOutput").ap())
    hybrid_step(nc, *args)
    r = _run(nc, [arrays], core_ids=[0])
    return tuple(r.results[0][f"out_{i}"] for i in range(len(_OUTS)))
```
